# Optimizing a Trainium2 kernel written in Bass

```python
import jax, jax.numpy as jnp
from jax import lax
import numpy as np

D_MODEL = 1024
BATCH = 1
SEQ = 512
DEPTH = 1

GRID_W = 64
CTX_LEN = 256
D_MIX = D_MODEL
GLA_WIDTH = D_MIX // 2
POOL_WIDTH = D_MIX - GLA_WIDTH
GLA_HEADS = 4
GLA_DV = GLA_WIDTH // GLA_HEADS
GLA_DK = GLA_DV // 2
GLA_QK = GLA_HEADS * GLA_DK
GATE_RANK = 16
GATE_NORMALIZER = 16.0
GLA_CHUNK = 64
POOL_GROUPS = 4
POOL_GC = POOL_WIDTH // POOL_GROUPS
POOL_WINDOWS = (2, 4, 8, 16)
N_EXPERTS = 32
TOP_K = 4
D_FF = D_MODEL
SWIGLU_LIMIT = 7.0
SWIGLU_ALPHA = 1.702
EXPERT_BLOCK = 128
N_MOD = 6
EPS = 1e-6
D_IN = 2 * GLA_QK + 2 * GLA_WIDTH + 2 * GATE_RANK + POOL_WIDTH
SPLIT_POINTS = (GLA_QK, 2 * GLA_QK, 2 * GLA_QK + GLA_WIDTH, 2 * GLA_QK + 2 * GLA_WIDTH,
                2 * GLA_QK + 2 * GLA_WIDTH + GATE_RANK, 2 * GLA_QK + 2 * GLA_WIDTH + 2 * GATE_RANK)


def rmsnorm(x, w):
    xf = x.astype(jnp.float32)
    var = jnp.mean(xf * xf, axis=-1, keepdims=True)
    return (xf * lax.rsqrt(var + EPS) * w.astype(jnp.float32)).astype(x.dtype)

def modulate(h, shift, scale):
    return h * (1.0 + scale) + shift

def to_heads(t, d):
    b_, n, _ = t.shape
    return t.reshape(b_, n, GLA_HEADS, d).transpose(0, 2, 1, 3).astype(jnp.float32)

def mixer_inputs(p, w_gk_f, b_gk_f, w_gk_b, b_gk_b):
    q, k, v, g, r_f, r_b, pool_in = jnp.split(p, SPLIT_POINTS, axis=-1)
    gk_f = jax.nn.log_sigmoid((r_f @ w_gk_f + b_gk_f).astype(jnp.float32)) / GATE_NORMALIZER
    gk_b = jax.nn.log_sigmoid((r_b @ w_gk_b + b_gk_b).astype(jnp.float32)) / GATE_NORMALIZER
    return (to_heads(q, GLA_DK), to_heads(k, GLA_DK), to_heads(v, GLA_DV),
            to_heads(gk_f, GLA_DK), to_heads(gk_b, GLA_DK), g, pool_in)

def gla_chunked(q, k, v, gk, s0, with_output=True):
    b_, h_, t_, dk = q.shape
    dv = v.shape[-1]
    n_ch = t_ // GLA_CHUNK
    qc = q.reshape(b_, h_, n_ch, GLA_CHUNK, dk) * (dk ** -0.5)
    kc = k.reshape(b_, h_, n_ch, GLA_CHUNK, dk)
    vc = v.reshape(b_, h_, n_ch, GLA_CHUNK, dv)
    bcum = jnp.cumsum(gk.reshape(b_, h_, n_ch, GLA_CHUNK, dk), axis=3)
    b_last = bcum[:, :, :, -1:, :]
    u = jnp.einsum('bhnsk,bhnsv->bhnkv', kc * jnp.exp(b_last - bcum), vc)
    decay = jnp.exp(b_last[:, :, :, 0, :])

    def step(s, inp):
        d, un = inp
        return d[..., None] * s + un, s

    s_final, s_prev = lax.scan(step, s0, (jnp.moveaxis(decay, 2, 0), jnp.moveaxis(u, 2, 0)))
    if not with_output:
        return None, s_final
    s_prev = jnp.moveaxis(s_prev, 0, 2)
    b_mid = bcum[:, :, :, GLA_CHUNK // 2 - 1:GLA_CHUNK // 2, :]
    a = jnp.einsum('bhntk,bhnsk->bhnts', qc * jnp.exp(bcum - b_mid), kc * jnp.exp(b_mid - bcum))
    mask = jnp.tril(jnp.ones((GLA_CHUNK, GLA_CHUNK), dtype=bool))
    a = jnp.where(mask, a, 0.0)
    o = (jnp.einsum('bhnts,bhnsv->bhntv', a, vc)
         + jnp.einsum('bhntk,bhnkv->bhntv', qc * jnp.exp(bcum), s_prev))
    return o.reshape(b_, h_, t_, dv), s_final

def gla_bidir(q, k, v, gk_f, gk_b, s0_f, s0_b, with_output=True):
    flip = lambda t: jnp.flip(t, axis=2)
    o_f, s_f = gla_chunked(q, k, v, gk_f, s0_f, with_output)
    o_b, s_b = gla_chunked(flip(q), flip(k), flip(v), flip(gk_b), s0_b, with_output)
    o = o_f + flip(o_b) if with_output else None
    return o, s_f, s_b

def gla_output(o, g, w_norm):
    b_, _, n, _ = o.shape
    o = o.transpose(0, 2, 1, 3)
    o = o * lax.rsqrt(jnp.mean(o * o, axis=-1, keepdims=True) + EPS) * w_norm.astype(jnp.float32)
    gate = jax.nn.silu(g.astype(jnp.float32)).reshape(o.shape)
    return (o * gate).reshape(b_, n, GLA_WIDTH)

def window_bounds(pos, w, length):
    lo = w // 2
    hi = w - 1 - lo
    return jnp.clip(pos - lo, 0, length), jnp.clip(pos + hi + 1, 0, length)

def pool_grid(xp, rows):
    b_, n, _ = xp.shape
    xf = xp.astype(jnp.float32).reshape(b_, rows, GRID_W, POOL_GROUPS, POOL_GC)
    sat = jnp.pad(jnp.cumsum(jnp.cumsum(xf, axis=1), axis=2), ((0, 0), (1, 0), (1, 0), (0, 0), (0, 0)))
    r = jnp.arange(rows)
    col = jnp.arange(GRID_W)
    outs = []
    for gi, w in enumerate(POOL_WINDOWS):
        r0, r1 = window_bounds(r, w, rows)
        c0, c1 = window_bounds(col, w, GRID_W)
        s = sat[:, :, :, gi]
        s_r1, s_r0 = s[:, r1], s[:, r0]
        tot = s_r1[:, :, c1] - s_r0[:, :, c1] - s_r1[:, :, c0] + s_r0[:, :, c0]
        cnt = ((r1 - r0)[:, None] * (c1 - c0)[None, :]).astype(jnp.float32)
        outs.append(tot / cnt[None, :, :, None])
    mean = jnp.stack(outs, axis=3)
    return (mean - xf).reshape(b_, n, POOL_GROUPS, POOL_GC)

def pool_seq(xp):
    b_, n, _ = xp.shape
    xf = xp.astype(jnp.float32).reshape(b_, n, POOL_GROUPS, POOL_GC)
    cs = jnp.pad(jnp.cumsum(xf, axis=1), ((0, 0), (1, 0), (0, 0), (0, 0)))
    pos = jnp.arange(n)
    outs = []
    for gi, w in enumerate(POOL_WINDOWS):
        i0, i1 = window_bounds(pos, w, n)
        outs.append((cs[:, i1, gi] - cs[:, i0, gi]) / (i1 - i0).astype(jnp.float32)[None, :, None])
    return jnp.stack(outs, axis=2) - xf

def pool_project(pooled, w_pool, pool_scale):
    b_, n = pooled.shape[:2]
    y = jnp.einsum('bngc,gcd->bngd', pooled, w_pool.astype(jnp.float32)).reshape(b_, n, POOL_WIDTH)
    return y * pool_scale.astype(jnp.float32)

def moe(h, w_router, b_router, w_gu, b_gu, w_down, b_down):
    shp = h.shape
    xt = h.reshape(-1, D_MODEL)
    n_tok = xt.shape[0]
    n_assign = n_tok * TOP_K
    logits = (xt @ w_router + b_router).astype(jnp.float32)
    top_vals, top_idx = lax.top_k(logits, TOP_K)
    weights = jax.nn.softmax(top_vals, axis=-1)
    flat_e = top_idx.reshape(-1)
    flat_tok = jnp.repeat(jnp.arange(n_tok, dtype=jnp.int32), TOP_K)
    flat_w = weights.reshape(-1)
    order = jnp.argsort(flat_e)
    sorted_e = flat_e[order]
    counts = jnp.bincount(flat_e, length=N_EXPERTS)
    padded = (counts + EXPERT_BLOCK - 1) // EXPERT_BLOCK * EXPERT_BLOCK
    start_unpad = jnp.cumsum(counts) - counts
    pad_end = jnp.cumsum(padded)
    start_pad = pad_end - padded
    dest = start_pad[sorted_e] + (jnp.arange(n_assign) - start_unpad[sorted_e])
    n_pad = n_assign + N_EXPERTS * EXPERT_BLOCK
    n_blocks = n_pad // EXPERT_BLOCK
    buf_tok = jnp.full((n_pad,), n_tok, dtype=jnp.int32).at[dest].set(flat_tok[order])
    buf_w = jnp.zeros((n_pad,), jnp.float32).at[dest].set(flat_w[order])
    block_e = jnp.minimum(jnp.searchsorted(pad_end, jnp.arange(n_blocks) * EXPERT_BLOCK, side='right'),
                          N_EXPERTS - 1)
    x_pad = jnp.concatenate([xt, jnp.zeros((1, D_MODEL), xt.dtype)], axis=0)
    xb = x_pad[buf_tok].reshape(n_blocks, EXPERT_BLOCK, D_MODEL)

    def expert_block(args):
        xblk, e = args
        gu = xblk @ w_gu[e] + b_gu[e]
        gate, up = jnp.split(gu, 2, axis=-1)
        gate = jnp.minimum(gate, SWIGLU_LIMIT)
        up = jnp.clip(up, -SWIGLU_LIMIT, SWIGLU_LIMIT)
        act = (up + 1.0) * gate * jax.nn.sigmoid(SWIGLU_ALPHA * gate)
        return act @ w_down[e] + b_down[e]

    yb = lax.map(expert_block, (xb, block_e)).reshape(n_pad, D_MODEL)
    y = jnp.zeros((n_tok + 1, D_MODEL), yb.dtype).at[buf_tok].add(yb * buf_w[:, None].astype(yb.dtype))
    return y[:n_tok].reshape(shp)

def first_inputs(seed: int = 0) -> dict:
    key = jax.random.key(seed)
    ks = jax.random.split(key, 32)
    nrm = lambda k, shp, s: jax.random.normal(k, shp, jnp.float32) * s
    L, D, E = DEPTH, D_MODEL, N_EXPERTS
    return {
        "x": nrm(ks[0], (BATCH, SEQ, D), 1.0),
        "c": nrm(ks[1], (BATCH, D), 1.0),
        "ctx": nrm(ks[2], (BATCH, CTX_LEN, D), 1.0),
        "c_ctx": nrm(ks[3], (D,), 1.0),
        "w_ada": nrm(ks[4], (L, D, N_MOD * D), 0.5 * D ** -0.5),
        "b_ada": nrm(ks[5], (L, N_MOD * D), 0.02),
        "norm_mix_w": 1.0 + nrm(ks[6], (L, D), 0.02),
        "norm_mlp_w": 1.0 + nrm(ks[7], (L, D), 0.02),
        "w_in": nrm(ks[8], (L, D, D_IN), D ** -0.5),
        "w_gk_f": nrm(ks[9], (L, GATE_RANK, GLA_QK), GATE_RANK ** -0.5),
        "b_gk_f": jax.random.uniform(ks[10], (L, GLA_QK), jnp.float32, -2.0, 4.0),
        "w_gk_b": nrm(ks[11], (L, GATE_RANK, GLA_QK), GATE_RANK ** -0.5),
        "b_gk_b": jax.random.uniform(ks[12], (L, GLA_QK), jnp.float32, -2.0, 4.0),
        "gla_norm_w": 1.0 + nrm(ks[13], (L, GLA_DV), 0.02),
        "w_pool": nrm(ks[14], (L, POOL_GROUPS, POOL_GC, POOL_GC), POOL_GC ** -0.5),
        "pool_scale": 1.0 + nrm(ks[15], (L, POOL_WIDTH), 0.1),
        "w_out": nrm(ks[16], (L, D_MIX, D), D_MIX ** -0.5),
        "w_router": nrm(ks[17], (L, D, E), D ** -0.5),
        "b_router": nrm(ks[18], (L, E), 0.01),
        "w_gu": nrm(ks[19], (L, E, D, 2 * D_FF), D ** -0.5),
        "b_gu": nrm(ks[20], (L, E, 2 * D_FF), 0.02),
        "w_down": nrm(ks[21], (L, E, D_FF, D), D_FF ** -0.5),
        "b_down": nrm(ks[22], (L, E, D), 0.02),
        "final_norm_w": 1.0 + nrm(ks[23], (D,), 0.02),
    }

def first_block(x, c, ctx, c_ctx, w_ada, b_ada, norm_mix_w, norm_mlp_w, w_in, w_gk_f, b_gk_f, w_gk_b,
              b_gk_b, gla_norm_w, w_pool, pool_scale, w_out, w_router, b_router, w_gu, b_gu, w_down,
              b_down, final_norm_w):
    h, hc = x, ctx
    b_, n_lat, _ = x.shape
    rows = n_lat // GRID_W
    for l in range(DEPTH):
        last = l == DEPTH - 1
        mod_x = (jax.nn.silu(c) @ w_ada[l] + b_ada[l])[:, None, :]
        mod_c = jax.nn.silu(c_ctx) @ w_ada[l] + b_ada[l]
        sh1, sc1, g1, sh2, sc2, g2 = jnp.split(mod_x, N_MOD, axis=-1)
        csh1, csc1, cg1, csh2, csc2, cg2 = jnp.split(mod_c, N_MOD, axis=-1)

        p_x = modulate(rmsnorm(h, norm_mix_w[l]), sh1, sc1) @ w_in[l]
        p_c = modulate(rmsnorm(hc, norm_mix_w[l]), csh1, csc1) @ w_in[l]
        qx, kx, vx, gkfx, gkbx, gx, poolx = mixer_inputs(p_x, w_gk_f[l], b_gk_f[l], w_gk_b[l], b_gk_b[l])
        qc, kc, vc, gkfc, gkbc, gc, poolc = mixer_inputs(p_c, w_gk_f[l], b_gk_f[l], w_gk_b[l], b_gk_b[l])

        s0 = jnp.zeros((b_, GLA_HEADS, GLA_DK, GLA_DV), jnp.float32)
        o_c, s_f, s_b = gla_bidir(qc, kc, vc, gkfc, gkbc, s0, s0, with_output=not last)
        o_x, _, _ = gla_bidir(qx, kx, vx, gkfx, gkbx, s_f, s_b)

        mix_x = jnp.concatenate([gla_output(o_x, gx, gla_norm_w[l]),
                                 pool_project(pool_grid(poolx, rows), w_pool[l], pool_scale[l])], axis=-1)
        h = h + g1 * (mix_x.astype(h.dtype) @ w_out[l])

        if not last:
            mix_c = jnp.concatenate([gla_output(o_c, gc, gla_norm_w[l]),
                                     pool_project(pool_seq(poolc), w_pool[l], pool_scale[l])], axis=-1)
            hc = hc + cg1 * (mix_c.astype(hc.dtype) @ w_out[l])
            hc = hc + cg2 * moe(modulate(rmsnorm(hc, norm_mlp_w[l]), csh2, csc2),
                                w_router[l], b_router[l], w_gu[l], b_gu[l], w_down[l], b_down[l])

        h = h + g2 * moe(modulate(rmsnorm(h, norm_mlp_w[l]), sh2, sc2),
                         w_router[l], b_router[l], w_gu[l], b_gu[l], w_down[l], b_down[l])
    return rmsnorm(h, final_norm_w)


CHUNK = 64
D_MIX_2 = D_MODEL
N_GROUPS = 4
GW = D_MIX_2 // N_GROUPS
HEAD_DIM = 64
N_HEADS_GROUP = GW // HEAD_DIM
ATTN_LEFT_CHUNKS = 8
N_BAND = ATTN_LEFT_CHUNKS + 1
REL_CLIP = 256
ATTN_SCALE = HEAD_DIM ** -0.5
NEG_INF = -1e30
RWKV_W_RANK = 32
RWKV_A_RANK = 32
RWKV_G_RANK = 64
RWKV_GN_EPS = HEAD_DIM * 1e-5
LRU_CONV = 4
LRU_C = 8.0
LRU_BLOCKS = N_HEADS_GROUP
LRU_BLOCK_DIM = GW // LRU_BLOCKS
ATTN_COLS = 3 * GW
HGRN_COLS = 4 * GW
RWKV_COLS = 3 * GW + RWKV_W_RANK + RWKV_A_RANK + RWKV_G_RANK
LRU_COLS = 2 * GW
D_IN_2 = ATTN_COLS + HGRN_COLS + RWKV_COLS + LRU_COLS
MLP_HIDDEN = 4 * D_MODEL
RMS_EPS = 1e-6


def split_cols(t, sizes):
    offs = np.cumsum(sizes)[:-1].tolist()
    return jnp.split(t, offs, axis=-1)

def rms_norm(x, gain):
    xf = x.astype(jnp.float32)
    y = xf * lax.rsqrt(jnp.mean(xf * xf, axis=-1, keepdims=True) + RMS_EPS)
    return (y * gain.astype(jnp.float32)).astype(x.dtype)

def to_heads_2(t):
    return t.reshape(t.shape[0], t.shape[1], N_HEADS_GROUP, HEAD_DIM)

def to_chunks(t):
    b, s, _ = t.shape
    return t.reshape(b, s // CHUNK, CHUNK, N_HEADS_GROUP, HEAD_DIM).transpose(1, 0, 3, 2, 4)

def from_chunks(t):
    nc, b = t.shape[0], t.shape[1]
    return t.transpose(1, 0, 3, 2, 4).reshape(b, nc * CHUNK, GW)

def chunk_attention(q, k, v, rel_bias):
    b, s, _ = q.shape
    nc = s // CHUNK
    shp = (b, nc, CHUNK, N_HEADS_GROUP, HEAD_DIM)
    qc, kc, vc = q.reshape(shp), k.reshape(shp), v.reshape(shp)
    pad = ((0, 0), (ATTN_LEFT_CHUNKS, 0), (0, 0), (0, 0), (0, 0))
    band = jnp.arange(nc)[:, None] + jnp.arange(N_BAND)[None, :]
    kb = jnp.pad(kc, pad)[:, band].reshape(b, nc, N_BAND * CHUNK, N_HEADS_GROUP, HEAD_DIM)
    vb = jnp.pad(vc, pad)[:, band].reshape(b, nc, N_BAND * CHUNK, N_HEADS_GROUP, HEAD_DIM)
    scores = jnp.einsum('bcqhd,bckhd->bchqk', qc, kb) * ATTN_SCALE
    key_off = ((jnp.arange(N_BAND) - ATTN_LEFT_CHUNKS)[:, None] * CHUNK
               + jnp.arange(CHUNK)[None, :]).reshape(-1)
    rel = key_off[None, :] - jnp.arange(CHUNK)[:, None]
    bias = rel_bias.astype(jnp.float32)[:, jnp.clip(rel, -REL_CLIP, REL_CLIP) + REL_CLIP]
    valid = jnp.repeat(band >= ATTN_LEFT_CHUNKS, CHUNK, axis=1)
    scores = jnp.where(valid[None, :, None, None, :], scores + bias[None, None], NEG_INF)
    probs = jax.nn.softmax(scores, axis=-1)
    out = jnp.einsum('bchqk,bckhd->bcqhd', probs, vb)
    return out.reshape(b, s, GW)

def hgrn2(q_raw, f_raw, i_raw, g_raw, lb, norm_gain):
    b = q_raw.shape[0]
    log_f = jnp.logaddexp(jnp.log(lb), jnp.log1p(-lb) + jax.nn.log_sigmoid(f_raw))
    key = (1.0 - lb) * jax.nn.sigmoid(-f_raw)
    q = jax.nn.silu(q_raw)
    tri = jnp.tril(jnp.ones((CHUNK, CHUNK), dtype=bool))

    def step(state, inp):
        qc, kc, vc, gc = inp
        cum = jnp.cumsum(gc, axis=2)
        last = cum[:, :, -1:, :]
        o_inter = jnp.einsum('bhtk,bhkv->bhtv', qc * jnp.exp(cum), state)
        diff = cum[:, :, :, None, :] - cum[:, :, None, :, :]
        decay = jnp.exp(jnp.where(tri[None, None, :, :, None], diff, -jnp.inf))
        att = jnp.einsum('bhtk,bhsk,bhtsk->bhts', qc, kc, decay)
        o_intra = jnp.einsum('bhts,bhsv->bhtv', att, vc)
        new_state = (jnp.exp(last).transpose(0, 1, 3, 2) * state
                     + jnp.einsum('bhsk,bhsv->bhkv', kc * jnp.exp(last - cum), vc))
        return new_state, o_inter + o_intra

    state0 = jnp.zeros((b, N_HEADS_GROUP, HEAD_DIM, HEAD_DIM), jnp.float32)
    _, o = lax.scan(step, state0, (to_chunks(q), to_chunks(key), to_chunks(i_raw), to_chunks(log_f)))
    o = to_heads_2(from_chunks(o))
    o = o * lax.rsqrt(jnp.mean(o * o, axis=-1, keepdims=True) + RMS_EPS)
    return o.reshape(g_raw.shape) * norm_gain * jax.nn.silu(g_raw)

def rwkv7(pc, mu, w0, w2, a0, a2, g2, k_k, k_a, r_k, ln_w, ln_b):
    b, s, _ = pc.shape
    prev = jnp.pad(pc, ((0, 0), (1, 0), (0, 0)))[:, :-1]
    xs = pc + mu * (prev - pc)
    r, k, v, w_lo, a_lo, g_lo = split_cols(xs, [GW, GW, GW, RWKV_W_RANK, RWKV_A_RANK, RWKV_G_RANK])
    w_pre = -jax.nn.softplus(-(w0 + jnp.tanh(w_lo) @ w2)) - 0.5
    decay = jnp.exp(-jnp.exp(w_pre))
    a = jax.nn.sigmoid(a0 + a_lo @ a2)
    g = jax.nn.sigmoid(g_lo) @ g2
    kk = to_heads_2(k * k_k)
    kk = kk / jnp.maximum(jnp.sqrt(jnp.sum(kk * kk, axis=-1, keepdims=True)), 1e-12)
    k = k * (1.0 + (a - 1.0) * k_a)
    r_h, w_h, k_h, v_h, a_h = to_heads_2(r), to_heads_2(decay), to_heads_2(k), to_heads_2(v), to_heads_2(a)

    def step(state, inp):
        rt, wt, kt, vt, kkt, at = inp
        sa = jnp.einsum('bhvk,bhk->bhv', state, -kkt)
        state = (state * wt[:, :, None, :] + sa[..., None] * (kkt * at)[:, :, None, :]
                 + vt[..., None] * kt[:, :, None, :])
        return state, jnp.einsum('bhvk,bhk->bhv', state, rt)

    seq_first = lambda t: t.transpose(1, 0, 2, 3)
    state0 = jnp.zeros((b, N_HEADS_GROUP, HEAD_DIM, HEAD_DIM), jnp.float32)
    _, y = lax.scan(step, state0, (seq_first(r_h), seq_first(w_h), seq_first(k_h),
                                   seq_first(v_h), seq_first(kk), seq_first(a_h)))
    y = seq_first(y)
    mean = jnp.mean(y, axis=-1, keepdims=True)
    var = jnp.mean(jnp.square(y - mean), axis=-1, keepdims=True)
    y = ((y - mean) * lax.rsqrt(var + RWKV_GN_EPS)).reshape(b, s, GW) * ln_w + ln_b
    bonus = (jnp.sum(r_h * k_h * r_k, axis=-1, keepdims=True) * v_h).reshape(b, s, GW)
    return (y + bonus) * g

def rglru(xb, gb, conv_w, conv_b, wa, ba, wx, bx, lam):
    b, s, _ = xb.shape
    conv = lax.conv_general_dilated(xb, conv_w.astype(xb.dtype)[:, None, :], window_strides=(1,),
                                    padding=[(LRU_CONV - 1, 0)],
                                    dimension_numbers=('NWC', 'WIO', 'NWC'),
                                    feature_group_count=GW) + conv_b
    xh = conv.reshape(b, s, LRU_BLOCKS, LRU_BLOCK_DIM)
    gate_r = jax.nn.sigmoid(jnp.einsum('bsnd,nde->bsne', xh, wa).reshape(b, s, GW) + ba)
    gate_i = jax.nn.sigmoid(jnp.einsum('bsnd,nde->bsne', xh, wx).reshape(b, s, GW) + bx)
    log_a = -LRU_C * gate_r * jax.nn.softplus(-lam)
    a = jnp.exp(log_a)
    inp = jnp.sqrt(-jnp.expm1(2.0 * log_a)) * (gate_i * conv)

    def combine(c1, c2):
        a1, b1 = c1
        a2, b2 = c2
        return a1 * a2, a2 * b1 + b2

    _, h = lax.associative_scan(combine, (a, inp), axis=1)
    return h * jax.nn.gelu(gb)

def second_inputs(seed: int = 0) -> dict:
    key = jax.random.key(seed)
    ks = jax.random.split(key, 32)
    L = DEPTH

    def nrm(k, shape, scale):
        return jax.random.normal(k, shape, jnp.float32) * scale

    u = jax.random.uniform(ks[27], (L, GW), jnp.float32, 0.9, 0.999)
    a_root = u ** (1.0 / LRU_C)
    lam = jnp.log(a_root) - jnp.log1p(-a_root)
    return {
        'x': nrm(ks[0], (BATCH, SEQ, D_MODEL), 1.0),
        'norm_mix_pre': 1.0 + nrm(ks[1], (L, D_MODEL), 0.05),
        'norm_mix_post': 1.0 + nrm(ks[2], (L, D_MODEL), 0.05),
        'norm_mlp_pre': 1.0 + nrm(ks[3], (L, D_MODEL), 0.05),
        'norm_mlp_post': 1.0 + nrm(ks[4], (L, D_MODEL), 0.05),
        'w_in': nrm(ks[5], (L, D_MODEL, D_IN_2), D_MODEL ** -0.5),
        'w_out': nrm(ks[6], (L, D_MIX_2, D_MODEL), D_MIX_2 ** -0.5),
        'attn_rel_bias': nrm(ks[7], (L, N_HEADS_GROUP, 2 * REL_CLIP + 1), 0.2),
        'hgrn_lb_logits': nrm(ks[8], (L, GW), 0.5),
        'hgrn_norm': 1.0 + nrm(ks[9], (L, GW), 0.05),
        'rwkv_mu': jax.random.uniform(ks[10], (L, RWKV_COLS), jnp.float32, 0.2, 0.8),
        'rwkv_w0': jax.random.uniform(ks[11], (L, GW), jnp.float32, -6.0, 1.0),
        'rwkv_w2': nrm(ks[12], (L, RWKV_W_RANK, GW), 0.5 * RWKV_W_RANK ** -0.5),
        'rwkv_a0': nrm(ks[13], (L, GW), 0.1),
        'rwkv_a2': nrm(ks[14], (L, RWKV_A_RANK, GW), 0.5 * RWKV_A_RANK ** -0.5),
        'rwkv_g2': nrm(ks[15], (L, RWKV_G_RANK, GW), RWKV_G_RANK ** -0.5),
        'rwkv_k_k': 0.85 + nrm(ks[16], (L, GW), 0.05),
        'rwkv_k_a': 1.0 + nrm(ks[17], (L, GW), 0.05),
        'rwkv_r_k': nrm(ks[18], (L, N_HEADS_GROUP, HEAD_DIM), 0.1),
        'rwkv_ln_w': 1.0 + nrm(ks[19], (L, GW), 0.05),
        'rwkv_ln_b': nrm(ks[20], (L, GW), 0.02),
        'lru_conv_w': nrm(ks[21], (L, LRU_CONV, GW), 0.5 * LRU_CONV ** -0.5),
        'lru_conv_b': nrm(ks[22], (L, GW), 0.02),
        'lru_wa': nrm(ks[23], (L, LRU_BLOCKS, LRU_BLOCK_DIM, LRU_BLOCK_DIM), LRU_BLOCK_DIM ** -0.5),
        'lru_ba': nrm(ks[24], (L, GW), 0.02),
        'lru_wx': nrm(ks[25], (L, LRU_BLOCKS, LRU_BLOCK_DIM, LRU_BLOCK_DIM), LRU_BLOCK_DIM ** -0.5),
        'lru_bx': nrm(ks[26], (L, GW), 0.02),
        'lru_lambda': lam,
        'mlp_w1': nrm(ks[28], (L, D_MODEL, MLP_HIDDEN), D_MODEL ** -0.5),
        'mlp_w2': nrm(ks[29], (L, MLP_HIDDEN, D_MODEL), MLP_HIDDEN ** -0.5),
    }

def second_block(x, norm_mix_pre, norm_mix_post, norm_mlp_pre, norm_mlp_post, w_in, w_out,
              attn_rel_bias, hgrn_lb_logits, hgrn_norm, rwkv_mu, rwkv_w0, rwkv_w2, rwkv_a0, rwkv_a2,
              rwkv_g2, rwkv_k_k, rwkv_k_a, rwkv_r_k, rwkv_ln_w, rwkv_ln_b, lru_conv_w, lru_conv_b,
              lru_wa, lru_ba, lru_wx, lru_bx, lru_lambda, mlp_w1, mlp_w2):
    dt = x.dtype
    f32 = jnp.float32
    lb_sm = jax.nn.softmax(hgrn_lb_logits.astype(f32), axis=0)
    lb_all = jnp.maximum(jnp.cumsum(lb_sm, axis=0) - lb_sm[0:1], 0.0)
    for l in range(DEPTH):
        h = rms_norm(x, norm_mix_pre[l])
        proj = (h @ w_in[l]).astype(f32)
        pa, pb, pc, pd = split_cols(proj, [ATTN_COLS, HGRN_COLS, RWKV_COLS, LRU_COLS])
        qa, ka, va = split_cols(pa, [GW, GW, GW])
        ya = chunk_attention(qa, ka, va, attn_rel_bias[l])
        qb, fb, ib, gb = split_cols(pb, [GW, GW, GW, GW])
        yb = hgrn2(qb, fb, ib, gb, lb_all[l], hgrn_norm[l].astype(f32))
        yc = rwkv7(pc, rwkv_mu[l].astype(f32), rwkv_w0[l].astype(f32), rwkv_w2[l].astype(f32),
                   rwkv_a0[l].astype(f32), rwkv_a2[l].astype(f32), rwkv_g2[l].astype(f32),
                   rwkv_k_k[l].astype(f32), rwkv_k_a[l].astype(f32), rwkv_r_k[l].astype(f32),
                   rwkv_ln_w[l].astype(f32), rwkv_ln_b[l].astype(f32))
        xd, gd = split_cols(pd, [GW, GW])
        yd = rglru(xd, gd, lru_conv_w[l].astype(f32), lru_conv_b[l].astype(f32), lru_wa[l].astype(f32),
                   lru_ba[l].astype(f32), lru_wx[l].astype(f32), lru_bx[l].astype(f32),
                   lru_lambda[l].astype(f32))
        mix = jnp.concatenate([ya, yb, yc, yd], axis=-1).astype(dt)
        x = x + rms_norm(mix @ w_out[l], norm_mix_post[l])
        h = rms_norm(x, norm_mlp_pre[l])
        ff = jnp.square(jax.nn.relu(h @ mlp_w1[l])) @ mlp_w2[l]
        x = x + rms_norm(ff, norm_mlp_post[l])
    return x


def setup_inputs(seed=0):
    out = dict(first_inputs(seed))
    for name, value in second_inputs(seed + 1).items():
        if name != "x":
            out[name + "_2"] = value
    return out


def reference(
    x, c, ctx, c_ctx, w_ada, b_ada, norm_mix_w, norm_mlp_w, w_in, w_gk_f, b_gk_f, w_gk_b,
    b_gk_b, gla_norm_w, w_pool, pool_scale, w_out, w_router, b_router, w_gu, b_gu, w_down,
    b_down, final_norm_w, norm_mix_pre_2, norm_mix_post_2, norm_mlp_pre_2, norm_mlp_post_2,
    w_in_2, w_out_2, attn_rel_bias_2, hgrn_lb_logits_2, hgrn_norm_2, rwkv_mu_2, rwkv_w0_2,
    rwkv_w2_2, rwkv_a0_2, rwkv_a2_2, rwkv_g2_2, rwkv_k_k_2, rwkv_k_a_2, rwkv_r_k_2, rwkv_ln_w_2,
    rwkv_ln_b_2, lru_conv_w_2, lru_conv_b_2, lru_wa_2, lru_ba_2, lru_wx_2, lru_bx_2,
    lru_lambda_2, mlp_w1_2, mlp_w2_2,
):
    x = first_block(
        x, c, ctx, c_ctx, w_ada, b_ada, norm_mix_w, norm_mlp_w, w_in, w_gk_f, b_gk_f, w_gk_b,
        b_gk_b, gla_norm_w, w_pool, pool_scale, w_out, w_router, b_router, w_gu, b_gu, w_down,
        b_down, final_norm_w,
    )
    return second_block(
        x, norm_mix_pre_2, norm_mix_post_2, norm_mlp_pre_2, norm_mlp_post_2, w_in_2, w_out_2,
        attn_rel_bias_2, hgrn_lb_logits_2, hgrn_norm_2, rwkv_mu_2, rwkv_w0_2, rwkv_w2_2,
        rwkv_a0_2, rwkv_a2_2, rwkv_g2_2, rwkv_k_k_2, rwkv_k_a_2, rwkv_r_k_2, rwkv_ln_w_2,
        rwkv_ln_b_2, lru_conv_w_2, lru_conv_b_2, lru_wa_2, lru_ba_2, lru_wx_2, lru_bx_2,
        lru_lambda_2, mlp_w1_2, mlp_w2_2,
    )


_drawn_inputs = setup_inputs


def setup_inputs(seed=0):
    import zlib

    import numpy as np

    out = dict(_drawn_inputs(seed))
    spreads = {}
    factors = {'norm_mix_w': 3.553,
     'gla_norm_w': 6.421,
     'b_router': 20.713,
     'b_gu': 33.716,
     'b_down': 39.03,
     'attn_rel_bias_2': 2.909,
     'rwkv_w2_2': 4.448,
     'rwkv_a0_2': 2.799,
     'rwkv_ln_b_2': 5.35,
     'lru_ba_2': 64.0,
     'lru_bx_2': 41.637,
     'norm_mlp_w': 8.0}
    for name, (base, spread) in spreads.items():
        noise = np.random.default_rng([zlib.crc32(name.encode()), seed]).standard_normal(out[name].shape)
        drawn = base * np.exp(spread * noise) if base else spread * noise
        out[name] = __import__('jax').numpy.asarray(drawn.astype(out[name].dtype))
    for name, factor in factors.items():
        out[name] = (out[name] * factor).astype(out[name].dtype)
    return out
```

```python
from contextlib import ExitStack

import numpy as np
import concourse.bass as bass
from concourse import mybir

F32 = mybir.dt.float32
I32 = mybir.dt.int32
U32 = mybir.dt.uint32
BF16 = mybir.dt.bfloat16
ALU = mybir.AluOpType
ACT = mybir.ActivationFunctionType
AX_X = mybir.AxisListType.X

P = 128
D = 1024
KD = D // P
T = 512
TT = T // P
CTX = 256
TC = T + CTX
NT = TC // P
CH = 64
NCH = TC // CH
XCH = T // CH
EPS = 1e-6
SWIGLU_LIMIT = 7.0

VEC = {}
VEC_LIST = [("c", 8), ("c_ctx", 8), ("norm_mix_w", 8), ("norm_mlp_w", 8), ("gla_norm_w", 1),
            ("pool_scale", 4), ("b_gk_f", 2), ("b_gk_b", 2), ("norm_mix_pre_2", 8),
            ("norm_mlp_pre_2", 8), ("hgrn_norm_2", 2), ("rwkv_mu_2", 7), ("rwkv_w0_2", 2),
            ("rwkv_a0_2", 2), ("rwkv_k_k_2", 2), ("rwkv_k_a_2", 2), ("rwkv_r_k_2", 2),
            ("rwkv_ln_w_2", 2), ("rwkv_ln_b_2", 2), ("lru_conv_w_2", 8), ("lru_conv_b_2", 2),
            ("lru_ba_2", 2), ("lru_bx_2", 2), ("lru_lambda_2", 2)]
NVEC = 0
for _name, _rows in VEC_LIST:
    VEC[_name] = NVEC
    NVEC += _rows

SLOTS = 6
SLOT = 4096
ADA = range(12)
W_IN = [(0, 512), (512, 512), (1024, 512), (1536, 32), (1568, 512)]
W_IN2 = [(i * 512, 512) for i in range(6)] + [(3072, 128)]


class Weights:

    def __init__(self, nc, top, k, a):
        self.buf = k.W
        self.jobs = []
        self.first = {}

        def add(name, views, words):
            self.first[name] = len(self.jobs)
            self.jobs += [(v, w) for v, w in zip(views, words)]

        def cols(w, groups):
            v = w[0].rearrange("(k p) n -> p k n", p=P)
            return [v[:, :, c:c + n] for c, n in groups], [(KD, n) for c, n in groups]

        add("ada", *cols(a["w_ada"], [(i * 512, 512) for i in ADA]))
        add("in", *cols(a["w_in"], W_IN))
        add("out", *cols(a["w_out"], [(0, 512), (512, 512)]))
        self.before_moe = len(self.jobs)
        add("in2", *cols(a["w_in_2"], W_IN2))
        add("out2", *cols(a["w_out_2"], [(0, 512), (512, 512)]))
        add("mlp1", *cols(a["mlp_w1_2"], [(i * 512, 512) for i in range(8)]))
        w2 = a["mlp_w2_2"][0].rearrange("(g k p) n -> g p k n", k=4, p=P)
        add("mlp2", [w2[g] for g in range(8)], [(4, 1024)] * 8)
        self.loaded = [top.enter_context(nc.semaphore(f"weights_loaded_{s}")) for s in range(SLOTS)]
        self.used = top.enter_context(nc.semaphore("weights_used"))

    def tile(self, n):
        kk, w = self.jobs[n][1]
        s = n % SLOTS
        return self.buf[:, s * SLOT:s * SLOT + kk * w].rearrange("p (k n) -> p k n", k=kk)

    def load(self, sp, lo, hi):
        for n in range(lo, hi):
            if n >= SLOTS:
                sp.wait_ge(self.used, n - SLOTS + 1)
            sp.dma_start(self.tile(n), self.jobs[n][0]).then_inc(self.loaded[n % SLOTS], 16)

    def wait(self, pe, n):
        pe.wait_ge(self.loaded[n % SLOTS], 16 * (n // SLOTS + 1))


class Kit:

    def __init__(self, nc):
        self.nc = nc
        self.taken = []
        self.count = 0

    def semaphore(self, name):
        self.count += 1
        self.taken.append(self.nc.alloc_semaphore(name=f"{name}_{self.count}"))
        return self.taken[-1]

    def recycle_semaphores(self):
        self.nc.clear_and_free_semaphores(self.taken)
        self.nc.all_engine_barrier()
        self.taken = []


class Names:
    pass


def linker(eng, sem):
    count = [0]

    def link(ins):
        count[0] += 1
        ins.then_inc(sem, 1)
        eng.wait_ge(sem, count[0])
    return link


def phase_modulation(nc, k, a, w, xt):
    ps = k.ps
    with ExitStack() as st:
        sem = lambda n: k.semaphore(n)
        sb = lambda n, s, d=F32: st.enter_context(nc.sbuf_tensor(n, s, d))
        rows = sb("vec_rows", [P, P])
        rows2 = sb("vec_rows_2", [P, P])
        brows = sb("b_ada_rows", [48, P])
        bcol = sb("b_ada_cols", [P, 48])
        bg = sb("b_ada_gates", [P, 2, D])
        sil = sb("silu_c", [P, 2, KD])
        sig = sb("sigmoid_c", [P, 2, KD])
        both = sb("both_wide", [P, KD, P])
        xonly = sb("x_wide", [P, KD, P])
        mod = sb("mod_rows", [P, 4, D])
        c_in, rest_ready = sem("c_in"), sem("rest_ready")
        vec_in, vec_in_2, const_in, bg_in = sem("vec_in"), sem("vec_in_2"), sem("const_in"), sem("bg_in")
        tr, cols_done, sig_done, sil_done, wide = sem("tr"), sem("cols_done"), sem("sig_done"), sem("sil_done"), sem("wide")
        mm, ev, mtr, mcol, vch, done = sem("mm"), sem("ev"), sem("mtr"), sem("mcol"), sem("vch"), sem("mod_done")
        ones = sb("ones_blk", [P, P])
        junk, ms, rt = sb("sq_junk", [P, D]), sb("ms", [P, NT]), sb("rt", [P, NT])
        x_in, sq, msd, sd = sem("x_in"), sem("sq"), sem("mean_sq"), sem("sd")
        block = st.enter_context(nc.Block())

        @block.sync
        def _(sp):
            w.load(sp, 0, w.first["in"] + 5)

        @block.scalar
        def _(act):
            for name, r in VEC_LIST[0:2]:
                act.dma_start(rows[VEC[name]:VEC[name] + r, :], a["vec_views"][name]).then_inc(c_in, 16)
            act.dma_start(k.ident[:], a["const_ident"]).then_inc(c_in, 16)
            act.wait_ge(cols_done, 1)
            act.activation(sig[:], k.vec[:, 0:2 * KD].rearrange("p (a k) -> p a k", a=2), ACT.Sigmoid).then_inc(sig_done, 1)
            for name, r in VEC_LIST[2::2]:
                act.dma_start(rows2[VEC[name]:VEC[name] + r, :], a["vec_views"][name]).then_inc(vec_in, 16)
            act.dma_start(brows[:], a["b_ada"].rearrange("o (r p) -> (o r) p", p=P)).then_inc(vec_in, 16)
            act.dma_start(k.ones128[:], a["const_ones128"]).then_inc(const_in, 16)
            for i, g in enumerate((2, 5)):
                act.dma_start(bg[:, i, :], a["b_ada"][0:1, g * D:(g + 1) * D].to_broadcast([P, D])).then_inc(bg_in, 16)
            for i in range(NT):
                src = a["x"][0, i * P:(i + 1) * P, :] if i < TT else a["ctx"][0, (i - TT) * P:(i - TT + 1) * P, :]
                act.dma_start(xt[i], src).then_inc(x_in, 16)
            act.wait_ge(x_in, 16 * NT)
            for i in range(NT):
                act.activation(junk[:], xt[i], ACT.Square, accum_out=ms[:, i:i + 1]).then_inc(sq, 1)
                act.wait_ge(sq, i + 1)
            act.wait_ge(msd, 1)
            act.activation(rt[:], ms[:], ACT.Sqrt).then_inc(sd, 1)

        @block.gpsimd
        def _(pool):
            for name, r in VEC_LIST[3::2]:
                pool.dma_start(rows2[VEC[name]:VEC[name] + r, :], a["vec_views"][name]).then_inc(vec_in_2, 16)

        @block.tensor
        def _(pe):
            pe.wait_ge(c_in, 48)
            pe.transpose(ps[0][:, 0:2 * KD], rows[0:2 * KD, :], k.ident[0:2 * KD, 0:2 * KD]).then_inc(tr, 1)
            pe.wait_ge(wide, 1)
            for j, g in enumerate(ADA):
                if j == 4:
                    pe.wait_ge(vec_in, 16 * (len(VEC_LIST[2::2]) + 1))
                    pe.wait_ge(vec_in_2, 16 * len(VEC_LIST[3::2]))
                    pe.wait_ge(rest_ready, 1)
                    pe.wait_ge(const_in, 16)
                    pe.transpose(ps[7][:, 0:NVEC], rows2[0:NVEC, :], k.ident[0:NVEC, 0:NVEC])
                    pe.transpose(ps[7][:, P:P + 48], brows[:], k.ident[0:48, 0:48]).then_inc(tr, 1)
                n = w.first["ada"] + j
                w.wait(pe, n)
                if j >= 4:
                    pe.wait_ge(ev, j - 3)
                lhs = xonly if g // 2 in (2, 5) else both
                for kk in range(KD):
                    last = pe.matmul(ps[j % 4][:], lhs[:, kk, :], w.tile(n)[:, kk, :], start=kk == 0, stop=kk == KD - 1)
                last.then_inc(mm, 1)
                pe.wait_ge(mm, j + 1)
                pe.sem_inc(w.used, 1)
            pe.wait_ge(ev, 12)
            for i in range(4):
                for kk in range(KD):
                    last = pe.transpose(ps[4 + kk // 4][:, (kk % 4) * P:(kk % 4 + 1) * P], mod[:, i, kk * P:(kk + 1) * P], k.ident[:])
                    if kk % 4 == 3:
                        last.then_inc(mtr, 1)
                pe.wait_ge(mcol, 2 * (i + 1))

        @block.vector
        def _(dve):
            link = linker(dve, vch)
            dve.wait_ge(tr, 1)
            dve.tensor_copy(k.vec[:, 0:2 * KD], ps[0][:, 0:2 * KD]).then_inc(cols_done, 1)
            dve.memset(rows2[0:2 * KD, :], 0.0).then_inc(rest_ready, 1)
            link(dve.memset(ones[:], 1.0))
            dve.wait_ge(sig_done, 1)
            link(dve.tensor_tensor(sil[:], k.vec[:, 0:2 * KD].rearrange("p (a k) -> p a k", a=2), sig[:], ALU.mult))
            for kk in range(KD):
                dve.tensor_scalar(both[:, kk, 0:64], ones[:, 0:64], sil[:, 0, kk:kk + 1], None, ALU.mult)
                dve.tensor_scalar(both[:, kk, 64:P], ones[:, 0:64], sil[:, 1, kk:kk + 1], None, ALU.mult)
                last = dve.tensor_scalar(xonly[:, kk, :], ones[:], sil[:, 0, kk:kk + 1], None, ALU.mult)
            last.then_inc(wide, 1)
            dve.wait_ge(bg_in, 32)

            def norm_x():
                dve.wait_ge(tr, 2)
                link(dve.tensor_copy(k.vec[:, 2 * KD:NVEC], ps[7][:, 2 * KD:NVEC]))
                link(dve.tensor_copy(bcol[:], ps[7][:, P:P + 48]))
                dve.wait_ge(sq, NT)
                dve.tensor_scalar(ms[:], ms[:], 1.0 / D, EPS, ALU.mult, ALU.add).then_inc(msd, 1)
                dve.wait_ge(sd, 1)
                link(dve.reciprocal(rt[:], rt[:]))
                for i in range(NT):
                    dve.tensor_scalar(xt[i], xt[i], rt[:, i:i + 1], None, ALU.mult)

            for j, g in enumerate(ADA):
                if j == 6:
                    norm_x()
                dve.wait_ge(mm, j + 1)
                half = slice((g % 2) * 512, (g % 2) * 512 + 512)
                which = g // 2
                if which in (2, 5):
                    i = 0 if which == 2 else 1
                    dst = k.gate_rows[:, i, half]
                    dve.tensor_tensor(dst, ps[j % 4][:], bg[:, i, half], ALU.add).then_inc(ev, 1)
                else:
                    dst = mod[:, {0: 0, 1: 1, 3: 2, 4: 3}[which], half]
                    dve.tensor_copy(dst, ps[j % 4][:]).then_inc(ev, 1)
            for i, which in enumerate((0, 1, 3, 4)):
                for h in range(2):
                    dve.wait_ge(mtr, 2 * i + h + 1)
                    src = ps[4 + h][:].rearrange("p (k q c) -> p k q c", k=4, q=2)[:, :, :, 0]
                    b = bcol[:, which * 8 + h * 4:which * 8 + h * 4 + 4]
                    dve.tensor_tensor(k.modc[:, i, h * 4:h * 4 + 4, 0], src[:, :, 0], b, ALU.add)
                    dve.tensor_tensor(k.modc[:, i, h * 4:h * 4 + 4, 1], src[:, :, 1], b, ALU.add).then_inc(mcol, 1)
            dve.wait_ge(mcol, 8)
            nm = k.vec[:, VEC["norm_mix_w"]:VEC["norm_mix_w"] + 8]
            nl = k.vec[:, VEC["norm_mlp_w"]:VEC["norm_mlp_w"] + 8]
            for i, c, nw in ((1, 0, nm), (1, 1, nm), (3, 0, nl)):
                dve.scalar_tensor_tensor(out=k.modc[:, i, :, c], in0=k.modc[:, i, :, c], scalar=1.0, in1=nw, op0=ALU.add, op1=ALU.mult).then_inc(done, 1)
            dve.wait_ge(done, 3)


def phase_norm_in(nc, k, xt, hT):
    ps = k.ps
    with ExitStack() as st:
        tr, ev = k.semaphore("tr"), k.semaphore("ev")
        block = st.enter_context(nc.Block())

        @block.vector
        def _(dve):
            for j in range(2 * KD):
                kk, c = j // 2, j % 2
                n, lo = (T, 0) if c == 0 else (CTX, T)
                dve.wait_ge(tr, j + 1)
                dve.tensor_scalar(hT[:, kk, lo:lo + n], ps[j % 4][:, 0:n], k.modc[:, 1, kk, c:c + 1], k.modc[:, 0, kk, c:c + 1], ALU.mult, ALU.add).then_inc(ev, 1)

        @block.tensor
        def _(pe):
            for j in range(2 * KD):
                kk, c = j // 2, j % 2
                if j >= 4:
                    pe.wait_ge(ev, j - 3)
                for q, i in enumerate(range(TT) if c == 0 else range(TT, NT)):
                    last = pe.transpose(ps[j % 4][:, q * P:(q + 1) * P], xt[i][:, kk * P:(kk + 1) * P], k.ident[:])
                last.then_inc(tr, 1)


def project(nc, k, w, st, pe_jobs, banks, loads, prefetch):
    ps = k.ps
    sem = lambda n: k.semaphore(n)
    mm, ev_v, ev_a = sem("proj_mm"), sem("proj_ev_v"), sem("proj_ev_a")
    block = st.enter_context(nc.Block())

    @block.sync
    def _(sp):
        w.load(sp, *prefetch)

    @block.tensor
    def _(pe):
        for j, (n, kds, lhs, rhs, m, nn, dst, post) in enumerate(pe_jobs):
            w.wait(pe, n)
            if j >= banks:
                pe.wait_ge(ev_v if j % 2 == 0 else ev_a, (j - banks) // 2 + 1)
            for kk in range(kds):
                last = pe.matmul(ps[j % banks][0:m, 0:nn], lhs(kk), rhs(kk), start=kk == 0, stop=kk == kds - 1)
            last.then_inc(mm, 1)
            if j + 1 == len(pe_jobs) or pe_jobs[j + 1][0] != n:
                pe.wait_ge(mm, j + 1)
                pe.sem_inc(w.used, 1)

    @block.vector
    def _(dve):
        for j in range(0, len(pe_jobs), 2):
            n, kds, lhs, rhs, m, nn, dst, post = pe_jobs[j]
            dve.wait_ge(mm, j + 1)
            if post is None:
                dve.tensor_copy(dst, ps[j % banks][0:m, 0:nn]).then_inc(ev_v, 1)
            else:
                dve.tensor_scalar(dst, ps[j % banks][0:m, 0:nn], post, None, ALU.mult).then_inc(ev_v, 1)

    @block.scalar
    def _(act):
        for j in range(1, len(pe_jobs), 2):
            n, kds, lhs, rhs, m, nn, dst, post = pe_jobs[j]
            act.wait_ge(mm, j + 1)
            act.activation(dst, ps[j % banks][0:m, 0:nn], ACT.Copy, scale=1.0 if post is None else post).then_inc(ev_a, 1)


def phase_project_in(nc, k, a, w, hT, g):
    jobs = []
    L = w.first["in"]
    def feat(n, col, m, dst, lo, nn, post=None):
        jobs.append((n, KD, lambda kk, n=n, col=col, m=m: w.tile(n)[:, kk, col:col + m],
                     lambda kk, lo=lo, nn=nn: hT[:, kk, lo:lo + nn], m, nn, dst, post))
    for m in range(2):
        feat(L, m * P, P, g.qT[:, m, :], 0, T, 64.0 ** -0.5)
    for m in range(2):
        feat(L, 256 + m * P, P, g.kT[:, m, 0:T], 0, T)
        feat(L, 256 + m * P, P, g.kT[:, m, T:TC], T, CTX)
    for i in range(NT):
        jobs.append((L + 1, KD, lambda kk, i=i: hT[:, kk, i * P:(i + 1) * P],
                     lambda kk: w.tile(L + 1)[:, kk, :], P, 512, g.v[:, i, :], None))
    for m in range(4):
        feat(L + 2, m * P, P, g.gT[:, m, :], 0, T)
    feat(L + 3, 0, 32, g.rT[:, 0:T], 0, T)
    feat(L + 3, 0, 32, g.rT[:, T:TC], T, CTX)
    for m in range(4):
        feat(L + 4, m * P, P, g.poolT[:, m, :], 0, T)
    with ExitStack() as st:
        project(nc, k, w, st, jobs, 8, None, (L + 5, L + 7))


def scratch(k, slot, offset, *dims):
    lo = slot * SLOT + offset
    v = k.W[:, lo:lo + int(np.prod(dims))]
    if len(dims) == 1:
        return v
    names = "abcd"[:len(dims)]
    return v.rearrange(f"p ({' '.join(names)}) -> p {' '.join(names)}", **dict(zip(names, dims)))


def phase_gates(nc, k, a, g, t, pb):
    ps = k.ps
    z, e = scratch(k, 1, 0, 4, TC), scratch(k, 1, 3072, 4, TC)
    cum = t.cum
    with ExitStack() as st:
        sem = lambda n: k.semaphore(n)
        sb = lambda n, s, d=F32: st.enter_context(nc.sbuf_tensor(n, s, d))
        wgk = sb("wgk", [32, 2, 256])
        scanmask = sb("scan_mask", [P, TC])[:]
        w_in, wz, mm, zdone, e_ready, vch, ach = (sem(n) for n in ("wgk_in", "wgk_zero", "gk_mm", "z_done", "e_ready", "vch", "ach"))
        cum_done, dl, dm, ee, z_used = (sem(n) for n in ("cum_done", "d_last", "d_mid", "exp_done", "z_used"))
        block = st.enter_context(nc.Block())

        @block.sync
        def _(sp):
            pb.load(sp)
            sp.wait_ge(wz, 1)
            sp.dma_start(wgk[0:16, 0, :], a["w_gk_f"][0]).then_inc(w_in, 16)
            sp.dma_start(wgk[16:32, 1, :], a["w_gk_b"][0]).then_inc(w_in, 16)

        @block.gpsimd
        def _(pool):
            pool.memset(wgk[:], 0.0).then_inc(wz, 1)
            pb.groups(pool, (0, 1))

        @block.tensor
        def _(pe):
            pe.wait_ge(w_in, 32)
            for i in range(4):
                d, m = i // 2, i % 2
                for c, (lo, n) in enumerate(((0, T), (T, CTX))):
                    last = pe.matmul(ps[i * 2 + c][:, 0:n], wgk[:, d, m * P:(m + 1) * P], g.rT[:, lo:lo + n], start=True, stop=True)
                last.then_inc(mm, 1)

        @block.scalar
        def _(act):
            link = linker(act, ach)
            for i in range(4):
                act.wait_ge(mm, i + 1)
                b = k.vec[:, VEC["b_gk_f"] + i:VEC["b_gk_f"] + i + 1]
                for c, (lo, n) in enumerate(((0, T), (T, CTX))):
                    last = act.activation(z[:, i, lo:lo + n], ps[i * 2 + c][:, 0:n], ACT.Identity, bias=b)
            last.then_inc(zdone, 1)
            act.wait_ge(zdone, 1)
            link(act.activation(e, z, ACT.Abs))
            link(act.activation(e, e, ACT.Exp, scale=-1.0))
            act.activation(e, e, ACT.Ln, bias=1.0).then_inc(e_ready, 1)
            act.wait_ge(dl, 4)
            act.activation(t.elast[:], t.elast[:], ACT.Exp).then_inc(ee, 1)
            act.wait_ge(dm, 4)
            act.activation(t.einv, t.emid, ACT.Exp, scale=-1.0).then_inc(ee, 1)
            act.wait_ge(ee, 2)
            act.activation(t.emid, t.emid, ACT.Exp).then_inc(ee, 1)
            for d in range(2):
                last_pos = 63 if d == 0 else 0
                act.activation(t.decay[:, 2 * d:2 * d + 2, :], cum[:, 2 * d:2 * d + 2, last_pos::CH], ACT.Exp).then_inc(ee, 1)
            act.activation(t.eq, cum[:, :, 0:T], ACT.Exp).then_inc(ee, 1)

        @block.vector
        def _(dve):
            link = linker(dve, vch)
            link(dve.memset(scanmask, 1.0))
            link(dve.memset(scanmask[:, ::CH], 0.0))
            link(dve.memset(t.qmid, 0.0))
            link(dve.memset(t.qcum, 0.0))
            dve.wait_ge(e_ready, 1)
            link(dve.scalar_tensor_tensor(out=z, in0=z, scalar=0.0, in1=e, op0=ALU.min, op1=ALU.subtract))
            link(dve.tensor_scalar(z, z, 1.0 / 16.0, None, ALU.mult))
            for i in range(4):
                back = slice(None) if i < 2 else slice(None, None, -1)
                dve.tensor_tensor_scan(cum[:, i, back], scanmask, z[:, i, back], 0.0, ALU.mult, ALU.add).then_inc(cum_done, 1)
            dve.wait_ge(cum_done, 4)
            for i in range(4):
                lastp, midp = (63, 31) if i < 2 else (0, 32)
                cv = cum[:, i, :].rearrange("p (n c) -> p n c", c=CH)
                dve.tensor_tensor(t.elast[:, i, :].rearrange("p (n c) -> p n c", c=CH),
                                  cv[:, :, lastp:lastp + 1].to_broadcast([P, NCH, CH]), cv, ALU.subtract).then_inc(dl, 1)
            for i in range(4):
                lastp, midp = (63, 31) if i < 2 else (0, 32)
                cv = cum[:, i, 0:T].rearrange("p (n c) -> p n c", c=CH)
                dve.tensor_tensor(t.emid[:, i, :].rearrange("p (n c) -> p n c", c=CH),
                                  cv, cv[:, :, midp:midp + 1].to_broadcast([P, XCH, CH]), ALU.subtract).then_inc(dm, 1)
            dve.wait_ge(ee, 6)
            for d in range(2):
                dd = slice(2 * d, 2 * d + 2)
                dve.tensor_tensor(t.elast[:, dd, :], t.elast[:, dd, :], g.kT[:], ALU.mult)
                dve.tensor_tensor(t.einv[:, dd, :], t.einv[:, dd, :], g.kT[:, :, 0:T], ALU.mult)
                for par in range(2):
                    r = slice(64 * par, 64 * par + 64)
                    dve.tensor_tensor(t.qmid[r, dd, par, :], t.emid[r, dd, :], g.qT[r, :, :], ALU.mult)
                    link(dve.tensor_tensor(t.qcum[r, dd, par, :], t.eq[r, dd, :], g.qT[r, :, :], ALU.mult))


def phase_gla(nc, k, a, g, t, pb):
    ps = k.ps
    kd, A = t.kd, t.A
    with ExitStack() as st:
        sem = lambda n: k.semaphore(n)
        sb = lambda n, s, d=F32: st.enter_context(nc.sbuf_tensor(n, s, d))
        tr, kdone, u, sdone, sc, masked, summed, zeroed = (sem(n) for n in ("kd_tr", "kd_done", "u", "s_done", "scores", "masked", "a_sum", "zeroed"))
        o, sq, mean, msum, root, rst, fin, gs, vch, const_in, kused = (sem(n) for n in ("o", "o_sq", "mean", "msum", "root", "rst", "fin", "gsil", "vch", "const_in", "kd_read"))
        S = sb("S_ctx", [P, 2, 4, P])
        am = sb("a_masked", [P, 2, 2, P * 4])
        masks = sb("gla_masks", [P, 2, P], I32)
        osq = am[:, :, :, :].rearrange("p a b c -> p (a b) c")
        gsig = t.mixT[:, 0:4, :]
        block = st.enter_context(nc.Block())
        order = (list(range(XCH, NCH)) + list(range(XCH)), list(range(NCH - 1, XCH - 1, -1)) + list(range(XCH - 1, -1, -1)))

        def state(d, step):
            n = order[d][step] if step < NCH else None
            if n is None or n >= XCH:
                return S[:, step % 2, 2 * d:2 * d + 2, :]
            return t.S[:, n, 2 * d:2 * d + 2, :]

        @block.sync
        def _(sp):
            sp.dma_start(masks[:], a["const_gla_masks"]).then_inc(const_in, 16)

        @block.gpsimd
        def _(pool):
            pb.groups(pool, (2, 3))

        @block.tensor
        def _(pe):
            for i in range(NT):
                if i >= 2:
                    pe.wait_ge(kdone, i - 1)
                for q in range(4):
                    last = pe.transpose(ps[i % 2][:, q * P:(q + 1) * P], t.elast[:, q, i * P:(i + 1) * P], k.ident[:])
                last.then_inc(tr, 1)
            pe.wait_ge(kdone, NT)
            for step in range(NCH - 1):
                if step >= 2:
                    pe.wait_ge(sdone, 4 * (step - 1))
                for d in range(2):
                    n = order[d][step]
                    r = slice(64 * (n % 2), 64 * (n % 2) + 64)
                    for h in range(4):
                        last = pe.matmul(ps[2 + 2 * d + step % 2][64 * (h % 2):64 * (h % 2) + 64, (h // 2) * P:(h // 2 + 1) * P],
                                         kd[r, n // 2, 2 * d + h // 2, 64 * (h % 2):64 * (h % 2) + 64],
                                         g.v[r, n // 2, h * P:(h + 1) * P], start=True, stop=True)
                last.then_inc(u, 1)
            for i in range(TT):
                if i >= 1:
                    pe.wait_ge(masked, 2 * i)
                cols = slice(i * P, (i + 1) * P)
                for d in range(2):
                    for h in range(4):
                        last = pe.matmul(ps[d][:, h * P:(h + 1) * P], t.einv[:, 2 * d + h // 2, cols],
                                         t.qmid[:, 2 * d + h // 2, h % 2, cols], start=True, stop=True)
                last.then_inc(sc, 1)
            pe.wait_ge(summed, TT)
            pe.wait_ge(sdone, 4 * (NCH - 1))
            for h in range(4):
                for i in range(TT):
                    cols = slice(i * P, (i + 1) * P)
                    pe.matmul(ps[2 + h][:, cols], g.v[:, i, h * P:(h + 1) * P], A[:, i, h, :], start=True, stop=False, skip_group_check=True)
                    for c in range(2):
                        n = 2 * i + c
                        nc_cols = slice(n * CH, (n + 1) * CH)
                        for d in range(2):
                            last = pe.matmul(ps[2 + h][:, nc_cols], t.S[:, n, 2 * d + h // 2, :],
                                             t.qcum[:, 2 * d + h // 2, h % 2, nc_cols], start=False, stop=d == 1, skip_group_check=True)
                last.then_inc(o, 1)
            for h in range(4):
                pe.wait_ge(sq, h + 1)
                bank = ps[h % 2]
                if h >= 2:
                    pe.wait_ge(msum, h - 1)
                pe.matmul(bank[:], k.ones128[:], osq[:, h, :], start=True, stop=True).then_inc(mean, 1)

        @block.scalar
        def _(act):
            for i in range(NT):
                act.wait_ge(tr, i + 1)
                act.activation(kd[:, i, :, :].rearrange("p a b -> p (a b)"), ps[i % 2][:], ACT.Copy).then_inc(kdone, 1)
            act.activation(gsig, g.gT[:], ACT.Sigmoid).then_inc(gs, 1)
            act.wait_ge(summed, TT)
            for h in range(4):
                act.wait_ge(o, h + 1)
                act.activation(osq[:, h, :], ps[2 + h][:], ACT.Square).then_inc(sq, 1)
            act.wait_ge(msum, 4)
            act.activation(osq, osq, ACT.Sqrt).then_inc(root, 1)

        @block.vector
        def _(dve):
            link = linker(dve, vch)
            dve.memset(am[:], 0.0).then_inc(zeroed, 1)
            dve.memset(S[:, 0, :, :], 0.0).then_inc(zeroed, 1)
            dve.wait_ge(zeroed, 2)
            for step in range(NCH - 1):
                dve.wait_ge(u, step + 1)
                if step >= 1:
                    dve.wait_ge(sdone, 4 * step)
                for d in range(2):
                    n = order[d][step]
                    for m in range(2):
                        dve.scalar_tensor_tensor(out=state(d, step + 1)[:, m, :], in0=state(d, step)[:, m, :],
                                                 scalar=t.decay[:, 2 * d + m, n:n + 1],
                                                 in1=ps[2 + 2 * d + step % 2][:, m * P:(m + 1) * P],
                                                 op0=ALU.mult, op1=ALU.add).then_inc(sdone, 1)
            dve.wait_ge(const_in, 16)
            dve.wait_ge(kdone, NT)
            for i in range(TT):
                dve.wait_ge(sc, i + 1)
                for d in range(2):
                    dve.copy_predicated(am[:, i % 2, d, :].rearrange("p (h t) -> p h t", h=4),
                                        masks[:, d:d + 1, :].to_broadcast([P, 4, P]),
                                        ps[d][:].rearrange("p (h t) -> p h t", h=4)).then_inc(masked, 1)
                dve.wait_ge(masked, 2 * i + 2)
                dve.tensor_tensor(A[:, i, :, :].rearrange("p h t -> p (h t)"), am[:, i % 2, 0, :], am[:, i % 2, 1, :], ALU.add).then_inc(summed, 1)
            dve.wait_ge(gs, 1)
            link(dve.tensor_tensor(g.gT[:], g.gT[:], gsig, ALU.mult))
            for h in range(4):
                dve.wait_ge(mean, h + 1)
                dve.tensor_scalar(osq[:, h, :], ps[h % 2][:], EPS, None, ALU.add).then_inc(msum, 1)
            dve.wait_ge(root, 1)
            link(dve.reciprocal(osq, osq))
            wn = k.vec[:, VEC["gla_norm_w"]:VEC["gla_norm_w"] + 1]
            for h in range(4):
                link(dve.scalar_tensor_tensor(out=osq[:, h, :], in0=ps[2 + h][:], scalar=wn, in1=osq[:, h, :], op0=ALU.mult, op1=ALU.mult))
            for h in range(4):
                dve.tensor_tensor(t.mixT[:, h, :], osq[:, h, :], g.gT[:, h, :], ALU.mult).then_inc(fin, 1)
            dve.wait_ge(fin, 4)


class PoolBranch:
    GR, GC, PAD = 8, 64, 8

    def __init__(self, nc, k, a, g, t, st):
        sb = lambda n, s: st.enter_context(nc.sbuf_tensor(n, s, F32))
        self.g, self.a = g, a
        free = t.mixT[:, 4:8, :].rearrange("p a b -> p (a b)")
        nc_, nr = self.GR * (self.GC + 2 * self.PAD), (self.GR + 2 * self.PAD) * self.GC
        self.cols = [free[:, i * nc_:(i + 1) * nc_].rearrange("p (r c) -> p r c", r=self.GR) for i in range(2)]
        self.rows = [sb("pool_rows", [P, self.GR + 2 * self.PAD, self.GC])[:],
                     free[:, 0:nr].rearrange("p (r c) -> p r c", c=self.GC)]
        self.wp = sb("w_pool_sb", [P, 4, P])
        self.inv = scratch(k, 1, 14336, 4, T)
        self.loaded, self.pch = k.semaphore("pool_w_in"), k.semaphore("pch")
        self.link = linker(nc.gpsimd, self.pch)

    def load(self, sp):
        sp.dma_start(self.wp[:], self.a["w_pool"][0].rearrange("g c d -> c g d")).then_inc(self.loaded, 16)
        sp.dma_start(self.inv, self.a["const_pool_inv"].to_broadcast([P, 4, T])).then_inc(self.loaded, 16)

    def groups(self, pool, qs):
        link, cols, rows = self.link, self.cols, self.rows
        GR, GC, PAD = self.GR, self.GC, self.PAD
        pool.wait_ge(self.loaded, 32)
        for q in qs:
            half = 1 << q
            x = self.g.poolT[:, q, :].rearrange("p (r c) -> p r c", c=GC)
            link(pool.memset(cols[0], 0.0))
            link(pool.memset(rows[0], 0.0))
            link(pool.tensor_copy(cols[0][:, :, PAD:PAD + GC], x))
            src = 0
            for s in range(q + 1):
                n = GC + 2 * PAD - (2 << s) + 1
                link(pool.tensor_tensor(cols[1 - src][:, :, 0:n], cols[src][:, :, 0:n], cols[src][:, :, (1 << s):(1 << s) + n], ALU.add))
                src = 1 - src
            link(pool.tensor_copy(rows[0][:, PAD:PAD + GR, :], cols[src][:, :, PAD - half:PAD - half + GC]))
            src = 0
            for s in range(q + 1):
                n = GR + 2 * PAD - (2 << s) + 1
                link(pool.tensor_tensor(rows[1 - src][:, 0:n, :], rows[src][:, 0:n, :], rows[src][:, (1 << s):(1 << s) + n, :], ALU.add))
                src = 1 - src
            box = rows[src][:, PAD - half:PAD - half + GR, :]
            link(pool.tensor_tensor(box, box, self.inv[:, q, :].rearrange("p (r c) -> p r c", c=GC), ALU.mult))
            link(pool.tensor_tensor(x, box, x, ALU.subtract))


def phase_pool(nc, k, g, t, pb):
    ps = k.ps
    with ExitStack() as st:
        mm, ev = k.semaphore("pool_mm"), k.semaphore("pool_ev")
        block = st.enter_context(nc.Block())

        @block.tensor
        def _(pe):
            for q in range(4):
                pe.matmul(ps[q][:], pb.wp[:, q, :], g.poolT[:, q, :], start=True, stop=True).then_inc(mm, 1)

        @block.vector
        def _(dve):
            for q in range(4):
                dve.wait_ge(mm, q + 1)
                c = VEC["pool_scale"] + q
                dve.tensor_scalar(t.mixT[:, 4 + q, :], ps[q][:], k.vec[:, c:c + 1], None, ALU.mult).then_inc(ev, 1)
            dve.wait_ge(ev, 4)


def phase_out(nc, k, a, w, t, h):
    ps = k.ps
    with ExitStack() as st:
        sem = lambda n: k.semaphore(n)
        x_in, mm, ev, res = (sem(n) for n in ("x_in", "out_mm", "out_ev", "res"))
        tmp = scratch(k, 3, 0, 4, 512)
        block = st.enter_context(nc.Block())

        @block.sync
        def _(sp):
            for i in range(TT):
                sp.dma_start(h[:, i, :], a["x"][0, i * P:(i + 1) * P, :]).then_inc(x_in, 16)

        @block.tensor
        def _(pe):
            for half in range(2):
                n = w.first["out"] + half
                w.wait(pe, n)
                for i in range(TT):
                    for kk in range(KD):
                        last = pe.matmul(ps[half * 4 + i][:], t.mixT[:, kk, i * P:(i + 1) * P], w.tile(n)[:, kk, :], start=kk == 0, stop=kk == KD - 1)
                    last.then_inc(mm, 1)
                pe.wait_ge(mm, 4 * half + 4)
                pe.sem_inc(w.used, 1)

        @block.vector
        def _(dve):
            dve.wait_ge(x_in, 16 * TT)
            for j in range(8):
                half, i = j // 4, j % 4
                cols = slice(half * 512, half * 512 + 512)
                dve.wait_ge(mm, j + 1)
                if j >= 4:
                    dve.wait_ge(res, j - 3)
                dve.tensor_tensor(tmp[:, i, :], ps[j][:], k.gate_rows[:, 0, cols], ALU.mult).then_inc(ev, 1)
                dve.wait_ge(ev, j + 1)
                dve.tensor_tensor(h[:, i, cols], h[:, i, cols], tmp[:, i, :], ALU.add).then_inc(res, 1)
            dve.wait_ge(res, 8)


def constants():
    s, t = np.arange(P)[:, None], np.arange(P)[None, :]
    same = (s // CH) == (t // CH)
    inv = np.zeros((1, 4, T), np.float32)
    for q in range(4):
        wd = 2 << q
        lo, hi = wd // 2, wd - 1 - wd // 2
        cnt = lambda n: np.minimum(np.arange(n) + hi + 1, n) - np.maximum(np.arange(n) - lo, 0)
        inv[0, q] = (1.0 / (cnt(8)[:, None] * cnt(64)[None, :]).astype(np.float32)).reshape(T)
    return {
        "const_ident": np.eye(P, dtype=np.float32),
        "const_flip": np.ascontiguousarray(np.eye(P, dtype=np.float32)[::-1]),
        "const_ones128": np.full((P, P), 1.0 / P, np.float32),
        "const_gla_masks": np.stack([same & (s <= t), same & (s >= t)], 1).astype(np.int32),
        "const_pool_inv": inv,
        "const_ones64": same.astype(np.float32) / CH,
        "const_level_masks": np.stack([(s // (2 * l) == t // (2 * l)) & (s % (2 * l) < l) & (t % (2 * l) >= l) for l in (32, 16, 8, 4, 2, 1)]
                                      + [s == t], 1).astype(np.int32),
        "const_tri": np.stack([same & (s < t), same & (s <= t)], 1).astype(np.int32),
        "const_level_masks_f": np.stack([(s // (2 * l) == t // (2 * l)) & (s % (2 * l) < l) & (t % (2 * l) >= l) for l in (32, 16, 8, 4, 2, 1)], 1).astype(np.float32),
        "const_upper": (s < t).astype(np.float32),
        "const_iota": np.arange(E_, dtype=np.float32)[None, :],
        "const_tokens": (np.arange(P)[:, None] + P * np.arange(TT)[None, :]).astype(np.int32),
        "const_zero": np.zeros((P, MAX_BLOCKS), np.int32),
        "const_sel": (np.arange(96)[:, None] % E_ == np.arange(E_)[None, :]).astype(np.float32),
    }




def program(nc, a, out):
    k = Kit(nc)
    with ExitStack() as top:
        gsb = lambda n, s, d=F32: top.enter_context(nc.sbuf_tensor(n, s, d))
        k.W = gsb("W", [P, SLOTS * SLOT])
        k.ps = [top.enter_context(nc.psum_tensor(f"ps{i}", [P, 512], F32)) for i in range(8)]
        k.ident = gsb("ident", [P, P])
        k.vec = gsb("vec", [P, NVEC])
        k.modc = gsb("modc", [P, 4, KD, 2])
        k.gate_rows = gsb("gate_rows", [P, 2, D])
        k.ones128 = gsb("ones128", [P, P])
        w = Weights(nc, top, k, a)
        k.h = gsb("h", [P, TT, D])
        first_mixer(nc, k, a, w)
        moe_layer(nc, k, a, w)
        k.recycle_semaphores()
        second_block(nc, k, a, w, out)


def first_mixer(nc, k, a, w):
    with ExitStack() as s1:
        sb = lambda n, s, d=F32: s1.enter_context(nc.sbuf_tensor(n, s, d))
        g = Names()
        g.gT = sb("gT", [P, 4, T])
        flat = k.h[:].rearrange("p a b -> p (a b)")
        g.v = flat[:, 0:NT * 512].rearrange("p (i n) -> p i n", i=NT)
        g.qT = flat[:, NT * 512:NT * 512 + 2 * T].rearrange("p (m n) -> p m n", m=2)
        g.poolT = sb("poolT", [P, 4, T])
        g.kT = sb("kT", [P, 2, TC])
        g.rT = sb("rT", [32, TC])
        with ExitStack() as s2:
            ctx = s2.enter_context(nc.sbuf_tensor("ctx_tok", [P, NT - TT, D], F32))
            xt = [k.h[:, i, :] for i in range(TT)] + [ctx[:, i, :] for i in range(NT - TT)]
            phase_modulation(nc, k, a, w, xt)
            hT = s2.enter_context(nc.sbuf_tensor("hT", [P, KD, TC], F32))
            phase_norm_in(nc, k, xt, hT)
            phase_project_in(nc, k, a, w, hT, g)
        with ExitStack() as s3:
            t = Names()
            sb3 = lambda n, s, d=F32: s3.enter_context(nc.sbuf_tensor(n, s, d))
            t.elast = sb3("elast", [P, 4, TC])
            t.cum = sb3("cum", [P, 4, TC])
            t.mixT = sb3("mixT", [P, KD, T])
            t.decay = sb3("decay", [P, 4, NCH])
            t.emid, t.eq, t.einv = (scratch(k, 1, 2048 * i, 4, T) for i in range(3))
            t.qmid, t.qcum = (scratch(k, 1, 6144 + 4096 * i, 4, 2, T) for i in range(2))
            pb = PoolBranch(nc, k, a, g, t, s3)
            phase_gates(nc, k, a, g, t, pb)
            t.S = scratch(k, 1, 0, XCH, 4, P)
            t.kd = t.cum[:].rearrange("p a (i c) -> p (a i c)", c=P).rearrange("p (i q c) -> p i q c", i=NT, q=4)
            t.A = t.elast[:].rearrange("p a c -> p (a c)")[:, 0:2048].rearrange("p (i h t) -> p i h t", i=TT, h=4)
            phase_gla(nc, k, a, g, t, pb)
            phase_pool(nc, k, g, t, pb)
            phase_out(nc, k, a, w, t, k.h)



E_ = 32
TOPK = 4
MAX_BLOCKS = TOPK * T // P + E_ + 1
GU_Q = 4
CHUNKS = GU_Q + 2


def phase_route(nc, k, a, w, m, ex_w):
    ps = k.ps
    with ExitStack() as st:
        sem = lambda n: k.semaphore(n)
        sb = lambda n, s, d=F32: st.enter_context(nc.sbuf_tensor(n, s, d))
        xn = sb("xn_tok", [P, TT, D])
        xmT = sb("xmT", [P, KD, T])
        junk = sb("r_junk", [P, D])
        ms, rt = sb("r_ms", [P, TT]), sb("r_rt", [P, TT])
        wr = sb("w_router_sb", [P, KD, E_])
        br = sb("b_router_sb", [P, E_])
        ru = sb("route_upper", [P, P])
        ones = sb("route_ones", [P, P])
        iota, ebase = sb("iota_e", [P, E_]), sb("base_e", [P, E_])
        tokid = sb("tok_ids", [P, TT], I32)
        zero = sb("zero_tab", [P, MAX_BLOCKS], I32)
        logits = sb("logits", [P, TT, E_])
        vals, idx, idxf = sb("vals", [P, TT, 8]), sb("idx", [P, TT, 8], U32), sb("idxf", [P, TT, 8])
        hot, prod = sb("hot", [P, TT, TOPK, E_]), sb("hot_rank", [P, TT, TOPK, E_])
        M, R = sb("M", [P, TT, E_]), sb("R", [P, TT, E_])
        ex, ssum, destf = sb("ex", [P, TT, TOPK]), sb("ssum", [P, TT]), sb("destf", [P, TT, TOPK])
        nb, gt = sb("nb", [P, E_]), sb("gt", [P, E_])
        bias = sb("bias_f32", [96, 3 * D])
        bias_in, rounded, rest = sem("bias_in"), sem("bias_rounded"), sem("bias_rest")
        tabf, one_row = sb("tabf", [P, E_ + 2]), sb("one_row", [P, E_])
        c_in, sq, vch, sd, xnd, tr, ev, lg, cnt, xm, hots, tab0, exd, destd, scat, mx = (sem(n) for n in (
            "c_in", "r_sq", "vch", "r_sd", "r_xn", "r_tr", "r_ev", "lg", "rank_mm", "xn_out", "hots", "table_zero", "ex_done", "dest_done", "scattered", "max_sub"))
        block = st.enter_context(nc.Block())

        @block.sync
        def _(sp):
            for dst, src in ((wr[:], a["w_router"][0].rearrange("(k p) e -> p k e", p=P)), (br[:], a["b_router"].to_broadcast([P, E_])),
                             (ru[:], a["const_upper"]), (iota[:], a["const_iota"].to_broadcast([P, E_])),
                             (tokid[:], a["const_tokens"]), (zero[:], a["const_zero"])):
                sp.dma_start(dst, src).then_inc(c_in, 16)
            sp.wait_ge(c_in, 16 * 6)
            sp.dma_start(m.slot_token.rearrange("(p n) o -> p (n o)", p=P), zero[:]).then_inc(tab0, 16)
            for c in range(CHUNKS):
                ex_w.load(sp, 0, c)
            sp.wait_ge(xnd, TT)
            for i in range(TT):
                sp.dma_start(m.xn[i * P:(i + 1) * P, :], xn[:, i, :]).then_inc(xm, 16)
            sp.wait_ge(xm, 16 * TT)

        @block.scalar
        def _(act):
            for part in range(3):
                r = slice(32 * part, 32 * part + 32)
                act.dma_start(bias[r, 0:2 * D], a["b_gu"][0]).then_inc(bias_in, 16)
                act.dma_start(bias[r, 2 * D:3 * D], a["b_down"][0]).then_inc(bias_in, 16)
            act.dma_start(m.sel[:], a["const_sel"]).then_inc(bias_in, 16)
            for i in range(TT):
                act.activation(junk[:], k.h[:, i, :], ACT.Square, accum_out=ms[:, i:i + 1]).then_inc(sq, 1)
                act.wait_ge(sq, i + 1)
            act.wait_ge(vch, 1)
            act.activation(rt[:], ms[:], ACT.Sqrt).then_inc(sd, 1)
            act.wait_ge(bias_in, 16 * 7)
            act.activation(m.bias[:], bias[:], ACT.Copy).then_inc(rounded, 1)
            act.wait_ge(rest, 1)
            act.activation(m.bias[32:64, :], bias[32:64, :], ACT.Copy).then_inc(rounded, 1)
            act.activation(m.bias[64:96, :], bias[64:96, :], ACT.Copy).then_inc(rounded, 1)
            act.wait_ge(mx, 1)
            act.activation(ex[:], ex[:], ACT.Exp).then_inc(exd, 1)
            act.wait_ge(rest, 2)
            act.activation(m.bias[64:96, :], bias[64:96, :], ACT.Copy).then_inc(rounded, 1)

        @block.tensor
        def _(pe):
            pe.wait_ge(xnd, TT)
            for j in range(KD):
                if j >= 4:
                    pe.wait_ge(ev, j - 3)
                for i in range(TT):
                    last = pe.transpose(ps[j % 4][:, i * P:(i + 1) * P], xn[:, i, j * P:(j + 1) * P], k.ident[:])
                last.then_inc(tr, 1)
            pe.wait_ge(ev, KD)
            pe.wait_ge(c_in, 16 * 6)
            for i in range(TT):
                for kk in range(KD):
                    last = pe.matmul(ps[4][:, i * E_:(i + 1) * E_], xmT[:, kk, i * P:(i + 1) * P], wr[:, kk, :], start=kk == 0, stop=kk == KD - 1)
            last.then_inc(lg, 1)
            pe.wait_ge(hots, 1)
            for i in range(TT + 1):
                for j in range(min(i + 1, TT)):
                    last = pe.matmul(ps[5][:, i * E_:(i + 1) * E_], ru[:] if j == i else ones[:], M[:, j, :], start=j == 0, stop=j == min(i, TT - 1))
            last.then_inc(cnt, 1)

        @block.vector
        def _(dve):
            link = linker(dve, vch)
            dve.wait_ge(sq, TT)
            link(dve.tensor_scalar(ms[:], ms[:], 1.0 / D, EPS, ALU.mult, ALU.add))
            dve.wait_ge(sd, 1)
            link(dve.reciprocal(rt[:], rt[:]))
            for i in range(TT):
                dve.tensor_scalar(xn[:, i, :], k.h[:, i, :], rt[:, i:i + 1], None, ALU.mult).then_inc(xnd, 1)
            link(dve.memset(ones[:], 1.0))
            for j in range(KD):
                dve.wait_ge(tr, j + 1)
                dve.tensor_scalar(xmT[:, j, :], ps[j % 4][:], k.modc[:, 3, j, 0:1], k.modc[:, 2, j, 0:1], ALU.mult, ALU.add).then_inc(ev, 1)
            dve.wait_ge(rounded, 1)
            dve.tensor_tensor(bias[:], bias[:], m.bias[:], ALU.subtract).then_inc(rest, 1)
            dve.wait_ge(lg, 1)
            link(dve.tensor_tensor(logits[:], ps[4][:, 0:TT * E_].rearrange("p (i e) -> p i e", i=TT), br[:, :].rearrange("p (o e) -> p o e", o=1).to_broadcast([P, TT, E_]), ALU.add))
            for i in range(TT):
                link(dve.max(vals[:, i, :], logits[:, i, :]))
                link(dve.max_index(idx[:, i, :], vals[:, i, :], logits[:, i, :]))
            link(dve.tensor_copy(idxf[:], idx[:]))
            dve.tensor_tensor(ex[:], vals[:, :, 0:TOPK], vals[:, :, 0:1].to_broadcast([P, TT, TOPK]), ALU.subtract).then_inc(mx, 1)
            for i in range(TT):
                last = dve.tensor_tensor(hot[:, i, :, :], iota[:, :].rearrange("p (o e) -> p o e", o=1).to_broadcast([P, TOPK, E_]),
                                         idxf[:, i, 0:TOPK].rearrange("p (q o) -> p q o", o=1).to_broadcast([P, TOPK, E_]), ALU.is_equal)
            link(last)
            link(dve.tensor_tensor(M[:], hot[:, :, 0, :], hot[:, :, 1, :], ALU.add))
            link(dve.tensor_tensor(M[:], M[:], hot[:, :, 2, :], ALU.add))
            dve.tensor_tensor(M[:], M[:], hot[:, :, 3, :], ALU.add).then_inc(hots, 1)
            dve.wait_ge(rounded, 3)
            dve.tensor_tensor(bias[64:96, :], bias[64:96, :], m.bias[64:96, :], ALU.subtract).then_inc(rest, 1)
            dve.wait_ge(exd, 1)
            link(dve.tensor_reduce(ssum[:], ex[:], AX_X, ALU.add))
            link(dve.reciprocal(ssum[:], ssum[:]))
            link(dve.tensor_tensor(m.weights[:], ex[:], ssum[:].rearrange("p (i o) -> p i o", o=1).to_broadcast([P, TT, TOPK]), ALU.mult))
            dve.wait_ge(cnt, 1)
            counts = ps[5][:, TT * E_:(TT + 1) * E_]
            link(dve.memset(nb[:], 1.0))
            for j in range(1, T // P):
                link(dve.tensor_scalar(gt[:], counts, float(j * P), None, ALU.is_gt))
                link(dve.tensor_tensor(nb[:], nb[:], gt[:], ALU.add))
            link(dve.memset(one_row[:], 1.0))
            link(dve.memset(tabf[:], 0.0))
            link(dve.tensor_tensor_scan(tabf[:, 1:E_ + 1], one_row[:], nb[:], 0.0, ALU.mult, ALU.add))
            link(dve.tensor_scalar(tabf[:, E_ + 1:E_ + 2], tabf[:, E_:E_ + 1], -1.0, float(MAX_BLOCKS), ALU.mult, ALU.add))
            link(dve.tensor_copy(m.table[:], tabf[0:1, :]))
            link(dve.tensor_copy(m.own[:], nb[0:1, :]))
            link(dve.tensor_scalar(ebase[:], tabf[:, 0:E_], float(P), None, ALU.mult))
            link(dve.tensor_tensor(R[:], ps[5][:, 0:TT * E_].rearrange("p (i e) -> p i e", i=TT), ebase[:, :].rearrange("p (o e) -> p o e", o=1).to_broadcast([P, TT, E_]), ALU.add))
            for i in range(TT):
                last = dve.tensor_tensor(prod[:, i, :, :], hot[:, i, :, :], R[:, i:i + 1, :].to_broadcast([P, TOPK, E_]), ALU.mult)
            link(last)
            link(dve.tensor_reduce(destf[:], prod[:], AX_X, ALU.add))
            dve.tensor_copy(m.dest[:], destf[:]).then_inc(destd, 1)
        @block.gpsimd
        def _(pool):
            pool.wait_ge(c_in, 16 * 6)
            pool.wait_ge(tab0, 16)
            pool.wait_ge(destd, 1)
            for i in range(TT):
                for q in range(TOPK):
                    pool.indirect_dma_start(m.slot_token, bass.IndirectOffsetOnAxis(ap=m.dest[:, i, q:q + 1], axis=0), tokid[:, i:i + 1], None).then_inc(scat, 16)
            pool.wait_ge(scat, 16 * TT * TOPK)



class Experts:

    def __init__(self, nc, k, a, w):
        self.n0 = w.before_moe
        self.W = k.W
        self.w = w
        self.gu = a["w_gu"][0].rearrange("e (k p) (s q n) -> e q s p k n", p=P, s=2, q=GU_Q)
        self.down = a["w_down"][0].rearrange("e (c k p) n -> e c p k n", c=2, p=P)
        self.landed = [k.semaphore(f"expert_chunk_{c}") for c in range(CHUNKS)]
        self.per_expert = [32] * GU_Q + [16] * 2

    def view(self, c):
        s = (self.n0 + c) % SLOTS
        v = self.W[:, s * SLOT:(s + 1) * SLOT]
        return v.rearrange("p (k s n) -> p k s n", k=KD, s=2) if c < GU_Q else v.rearrange("p (k n) -> p k n", k=4)

    def load(self, sp, e, c):
        if c < GU_Q:
            for s in range(2):
                sp.dma_start(self.view(c)[:, :, s, :], self.gu[e, c, s]).then_inc(self.landed[c], 16)
        else:
            sp.dma_start(self.view(c), self.down[e, c - GU_Q]).then_inc(self.landed[c], 16)


def phase_moe(nc, k, a, w, m, ex):
    ps = k.ps
    with ExitStack() as st:
        sem = lambda n: k.semaphore(n)
        sb = lambda n, s, d=F32: st.enter_context(nc.sbuf_tensor(n, s, d))
        rows_idx = sb("rows_idx", [P, 1], I32)
        xg = sb("x_rows", [P, D])
        xT, x_next = sb("x_turned", [P, KD, P]), sb("x_turned_next", [P, KD, P])
        sel = sb("bias_sel", [96, P], BF16)
        gate, sig, up = sb("gate", [P, 2, 256]), sb("sig", [P, 2, 256]), sb("up", [P, 2, 256])
        hid = sb("hidden", [P, GU_Q, 256])
        hT = sb("hidden_turned", [P, KD, P])
        yb = sb("y_rows", [P, D])
        idx_in, x_in, x_turn, x_ready, sel_ready, used = (sem(n) for n in ("idx_in", "x_rows_in", "x_turn", "x_ready", "sel_ready", "chunks_used"))
        zero_rows, zero_out, gathers, x_placed = sem("zero_rows"), sem("zero_out"), sem("gathers"), sem("x_placed")
        gated, sigd, upd, prod, hid_ready, h_turn, h_ready, y_ready, y_out = (sem(n) for n in ("gated", "sig_done", "up_done", "prod", "hid_ready", "h_turn", "h_ready", "y_ready", "y_out"))
        block = st.enter_context(nc.Block())

        def blocks(eng, e):
            lo = eng.value_load(m.table[0:1, bass.ds(e, 1)], min_val=0, max_val=44)
            own = eng.value_load(m.own[0:1, bass.ds(e, 1)], min_val=1, max_val=T // P)
            return lo, own

        @block.sync
        def _(sp):
            with sp.Fori(1, E_) as e:
                lo = sp.value_load(m.table[0:1, bass.ds(e, 1)], min_val=1, max_val=47)
                base = sp.snap(lo * 6)
                for c in range(CHUNKS):
                    sp.wait_ge(used, base + (c + 1))
                    ex.load(sp, e, c)
            last = sp.value_load(m.table[0:1, E_:E_ + 1], min_val=E_, max_val=48)
            for c in range(SLOTS):
                sp.wait_ge(used, last * 6 + (c + 1))
                n = w.first["in2"] + c
                sp.dma_start(w.tile(n), w.jobs[n][0]).then_inc(w.loaded[n % SLOTS], 16)

        @block.gpsimd
        def _(pool):
            pool.memset(yb[:], 0.0).then_inc(zero_rows, 1)
            pool.wait_ge(zero_rows, 1)
            end = pool.value_load(m.table[0:1, E_:E_ + 1], min_val=E_, max_val=MAX_BLOCKS - 1)
            with pool.Fori(end, MAX_BLOCKS) as g:
                pool.dma_start(m.y[bass.ds(g * P, P), :], yb[:]).then_inc(zero_out, 16)
            with pool.Fori(0, E_) as e:
                lo, own = blocks(pool, e)
                with pool.Fori(0, own) as j_e:
                    g = pool.snap(lo + j_e)
                    pool.dma_start(rows_idx[:], m.slot_token[bass.ds(g * P, P), :]).then_inc(idx_in, 16)
                    pool.wait_ge(idx_in, g * 16 + 16)
                    pool.wait_ge(x_turn, g * 2 + 2)
                    pool.sem_inc(gathers, 1)
                    pool.indirect_dma_start(xg[:], None, m.xn, bass.IndirectOffsetOnAxis(ap=rows_idx[:, 0:1], axis=0)).then_inc(x_in, 16)
                    pool.wait_ge(x_in, g * 16 + 16)
            last = pool.value_load(m.table[0:1, E_:E_ + 1], min_val=E_, max_val=MAX_BLOCKS - 1)
            left = pool.value_load(m.table[0:1, E_ + 1:E_ + 2], min_val=1, max_val=MAX_BLOCKS - E_)
            pool.wait_ge(x_turn, last * 2 + 2)
            pool.sem_inc(gathers, 1)
            pool.indirect_dma_start(xg[:], None, m.xn, bass.IndirectOffsetOnAxis(ap=rows_idx[:, 0:1], axis=0)).then_inc(x_in, 16)
            pool.wait_ge(zero_out, left * 16)

        @block.tensor
        def _(pe):
            def down(q, e, g):
                pe.wait_ge(h_ready, g * 4 + (q + 1))
                if q % 2 == 0:
                    pe.wait_ge(ex.landed[GU_Q + q // 2], e * 16 + 16)
                if q == 0:
                    pe.wait_ge(y_ready, g * 2 + 2)
                for t in (2 * q, 2 * q + 1):
                    for half in range(2):
                        last = pe.matmul(ps[4 + half][:], hT[:, t, :], ex.view(GU_Q + t // 4)[:, t % 4, half * 512:(half + 1) * 512],
                                         start=t == 0, stop=False)
                if q == 1:
                    last.then_inc(used, 1)
                if q == GU_Q - 1:
                    for half in range(2):
                        last = pe.matmul(ps[4 + half][:], sel[:], m.bias[:, 2 * D + half * 512:2 * D + (half + 1) * 512], start=False, stop=True)
                    last.then_inc(used, 1)

            def turn_x():
                for j in range(2):
                    for q in range(4):
                        kk = 4 * j + q
                        last = pe.transpose(ps[6 + j][:, q * P:(q + 1) * P], xg[:, kk * P:(kk + 1) * P], k.ident[:])
                    last.then_inc(x_turn, 1)

            def turn_hidden(q, g):
                pe.wait_ge(hid_ready, g * 4 + (q + 1))
                for j in range(2):
                    last = pe.transpose(ps[6 + q % 2][:, j * P:(j + 1) * P], hid[:, q, j * P:(j + 1) * P], k.ident[:])
                last.then_inc(h_turn, 1)

            pe.sem_inc(used, CHUNKS)
            pe.sem_inc(x_turn, 2)
            pe.wait_ge(x_in, 16)
            turn_x()
            with pe.Fori(0, E_) as e:
                lo, own = blocks(pe, e)
                with pe.Fori(0, own) as j_e:
                    g = pe.snap(lo + j_e)
                    pe.wait_ge(x_placed, g + 1)
                    for q in range(GU_Q):
                        pe.wait_ge(ex.landed[q], e * 32 + 32)
                        for kk in range(KD):
                            pe.matmul(ps[q][:], xT[:, kk, :], ex.view(q)[:, kk, :, :].rearrange("p s n -> p (s n)"), start=kk == 0, stop=False)
                        if q == 0:
                            pe.wait_ge(sel_ready, g + 1)
                        gu_bias = m.bias[:, 0:2 * D].rearrange("p (s n) -> p s n", s=2)[:, :, q * 256:(q + 1) * 256]
                        pe.matmul(ps[q][:].rearrange("p (s n) -> p s n", s=2), sel[:], gu_bias, start=False, stop=True).then_inc(used, 1)
                        if q == 1:
                            pe.wait_ge(x_in, g * 16 + 32)
                            turn_x()
                        if q == 2:
                            pe.wait_ge(x_ready, g * 8 + 16)
                            turn_hidden(0, g)
                    for q in range(1, GU_Q):
                        turn_hidden(q, g)
                        down(q - 1, e, g)
                    down(GU_Q - 1, e, g)

        @block.scalar
        def _(act):
            def ready_x():
                for j in range(2):
                    for q in range(4):
                        kk = 4 * j + q
                        act.activation(x_next[:, kk, :], ps[6 + j][:, q * P:(q + 1) * P], ACT.Identity,
                                       bias=k.modc[:, 2, kk, 0:1], scale=k.modc[:, 3, kk, 0:1]).then_inc(x_ready, 1)

            def ready_hidden(q, g):
                act.wait_ge(h_turn, g * 4 + (q + 1))
                act.activation(hT[:, 2 * q:2 * q + 2, :].rearrange("p a b -> p (a b)"), ps[6 + q % 2][:, 0:256], ACT.Copy).then_inc(h_ready, 1)

            act.sem_inc(y_ready, 2)
            act.wait_ge(x_turn, 4)
            ready_x()
            left = act.value_load(m.table[0:1, E_ + 1:E_ + 2], min_val=1, max_val=MAX_BLOCKS - E_)
            with act.Fori(0, E_) as e:
                lo, own = blocks(act, e)
                with act.Fori(0, own) as j_e:
                    g = act.snap(lo + j_e)
                    for q in range(GU_Q):
                        act.wait_ge(gated, g * 4 + (q + 1))
                        act.activation(sig[:, q % 2, :], gate[:, q % 2, :], ACT.Sigmoid, scale=1.702).then_inc(sigd, 1)
                        if q == 1:
                            act.wait_ge(x_turn, g * 2 + 6)
                            ready_x()
                        if q == 2:
                            ready_hidden(0, g)
                    for q in range(1, GU_Q):
                        ready_hidden(q, g)
                    act.wait_ge(zero_out, left * 16)
                    act.wait_ge(used, g * 6 + 12)
                    act.activation(yb[:, 0:512], ps[4][:], ACT.Copy).then_inc(y_ready, 1)
                    act.activation(yb[:, 512:D], ps[5][:], ACT.Copy).then_inc(y_ready, 1)
                    act.wait_ge(y_ready, g * 2 + 4)
                    act.dma_start(m.y[bass.ds(g * P, P), :], yb[:]).then_inc(y_out, 16)
                    act.wait_ge(y_out, g * 16 + 16)

        @block.vector
        def _(dve):
            dve.wait_ge(x_ready, KD)
            dve.tensor_copy(xT[:], x_next[:]).then_inc(x_placed, 1)
            with dve.Fori(0, E_) as e:
                lo, own = blocks(dve, e)
                with dve.Fori(0, own) as j_e:
                    g = dve.snap(lo + j_e)
                    dve.wait_ge(used, g * 6 + 6)
                    dve.tensor_copy(sel[:], m.sel[:, bass.ds(e, 1)].to_broadcast([96, P])).then_inc(sel_ready, 1)
                    for q in range(GU_Q):
                        b = q % 2
                        dve.wait_ge(used, g * 6 + (q + 7))
                        dve.tensor_scalar(gate[:, b, :], ps[q][:, 0:256], SWIGLU_LIMIT, None, ALU.min).then_inc(gated, 1)
                        dve.tensor_scalar(up[:, b, :], ps[q][:, 256:512], SWIGLU_LIMIT, -SWIGLU_LIMIT, ALU.min, ALU.max).then_inc(upd, 1)
                        dve.wait_ge(upd, g * 4 + (q + 1))
                        dve.wait_ge(gated, g * 4 + (q + 1))
                        dve.scalar_tensor_tensor(out=up[:, b, :], in0=up[:, b, :], scalar=1.0, in1=gate[:, b, :], op0=ALU.add, op1=ALU.mult).then_inc(prod, 1)
                        dve.wait_ge(prod, g * 4 + (q + 1))
                        dve.wait_ge(sigd, g * 4 + (q + 1))
                        dve.tensor_tensor(hid[:, q, :], up[:, b, :], sig[:, b, :], ALU.mult).then_inc(hid_ready, 1)
                    dve.wait_ge(x_ready, g * 8 + 16)
                    dve.tensor_copy(xT[:], x_next[:]).then_inc(x_placed, 1)



def phase_combine(nc, k, a, w, m):
    with ExitStack() as st:
        sem = lambda n: k.semaphore(n)
        sb = lambda n, s, d=F32: st.enter_context(nc.sbuf_tensor(n, s, d))
        NB = 6
        rows = sb("y_gathered", [P, NB, D])
        acc = sb("y_acc", [P, TT, D])
        fw = sb("final_w", [P, D])
        junk = sb("c_junk", [P, D])
        ms, rt = sb("c_ms", [P, TT]), sb("c_rt", [P, TT])
        got = [sem(f"got_{b}") for b in range(NB)]
        fin, added, vch, sq, sd = (sem(n) for n in ("fw_in", "added", "vch", "c_sq", "c_sd"))
        hd = sem("h_done")
        block = st.enter_context(nc.Block())

        @block.sync
        def _(sp):
            sp.dma_start(fw[:], a["final_norm_w"].rearrange("(o d) -> o d", o=1).to_broadcast([P, D])).then_inc(fin, 16)

        @block.gpsimd
        def _(pool):
            for j in range(TT * TOPK):
                if j >= NB:
                    pool.wait_ge(added, j - NB + 1)
                pool.indirect_dma_start(rows[:, j % NB, :], None, m.y, bass.IndirectOffsetOnAxis(ap=m.dest[:, j // TOPK, j % TOPK:j % TOPK + 1], axis=0)).then_inc(got[j % NB], 16)

        @block.vector
        def _(dve):
            link = linker(dve, vch)
            for j in range(TT * TOPK):
                i, q = j // TOPK, j % TOPK
                dve.wait_ge(got[j % NB], 16 * (j // NB + 1))
                wt = m.weights[:, i, q:q + 1]
                if q == 0:
                    dve.tensor_scalar(acc[:, i, :], rows[:, j % NB, :], wt, None, ALU.mult).then_inc(added, 1)
                else:
                    dve.scalar_tensor_tensor(out=acc[:, i, :], in0=rows[:, j % NB, :], scalar=wt, in1=acc[:, i, :], op0=ALU.mult, op1=ALU.add).then_inc(added, 1)
                dve.wait_ge(added, j + 1)
                if q == TOPK - 1:
                    link(dve.tensor_tensor(acc[:, i, :], acc[:, i, :], k.gate_rows[:, 1, :], ALU.mult))
                    dve.tensor_tensor(k.h[:, i, :], k.h[:, i, :], acc[:, i, :], ALU.add).then_inc(hd, 1)
            dve.wait_ge(sq, TT)
            link(dve.tensor_scalar(ms[:], ms[:], 1.0 / D, EPS, ALU.mult, ALU.add))
            dve.wait_ge(sd, 1)
            link(dve.reciprocal(rt[:], rt[:]))
            dve.wait_ge(fin, 16)
            for i in range(TT):
                link(dve.scalar_tensor_tensor(out=k.h[:, i, :], in0=k.h[:, i, :], scalar=rt[:, i:i + 1], in1=fw[:], op0=ALU.mult, op1=ALU.mult))

        @block.scalar
        def _(act):
            for i in range(TT):
                act.wait_ge(hd, i + 1)
                act.activation(junk[:], k.h[:, i, :], ACT.Square, accum_out=ms[:, i:i + 1]).then_inc(sq, 1)
                act.wait_ge(sq, i + 1)
            act.wait_ge(vch, TT + 1)
            act.activation(rt[:], ms[:], ACT.Sqrt).then_inc(sd, 1)




def moe_layer(nc, k, a, w):
    with ExitStack() as s1:
        sb = lambda n, s, d=F32: s1.enter_context(nc.sbuf_tensor(n, s, d))
        m = Names()
        m.xn = nc.dram_tensor("moe_xn", (T, D), F32).ap()
        m.slot_token = nc.dram_tensor("slot_token", (MAX_BLOCKS * P, 1), I32).ap()
        m.y = nc.dram_tensor("moe_y", (MAX_BLOCKS * P, D), F32).ap()
        m.table = sb("block_table", [1, E_ + 2], I32)
        m.own = sb("own_blocks", [1, E_], I32)
        m.dest = sb("dest", [P, TT, TOPK], I32)
        m.weights = sb("route_w", [P, TT, TOPK])
        m.bias = sb("bias_parts", [96, 3 * D], BF16)
        m.sel = sb("sel_cols", [96, E_])
        ex = Experts(nc, k, a, w)
        phase_route(nc, k, a, w, m, ex)
        phase_moe(nc, k, a, w, m, ex)
        phase_combine(nc, k, a, w, m)




RW_HD = 64


def phase_norm_turn(nc, k, tag, wrow, hT, room, prefetch=None):
    ps = k.ps
    with ExitStack() as st:
        sem = lambda n: k.semaphore(n + tag)
        sb = lambda n, s, d=F32: st.enter_context(nc.sbuf_tensor(n + tag, s, d))
        if room is None:
            xn, junk = sb("n_x", [P, TT, D]), sb("n_junk", [P, D])
        else:
            flat = room[:].rearrange("p a b -> p (a b)")
            xn, junk = flat[:, 0:TT * D].rearrange("p (i d) -> p i d", i=TT), flat[:, TT * D:(TT + 1) * D]
        ms, rt = sb("n_ms", [P, TT]), sb("n_rt", [P, TT])
        sq, vch, sd, xnd, tr, ev = (sem(n) for n in ("n_sq", "vch", "n_sd", "n_xn", "n_tr", "n_ev"))
        block = st.enter_context(nc.Block())

        if prefetch:
            block.sync(prefetch)

        @block.scalar
        def _(act):
            for i in range(TT):
                act.activation(junk[:], k.h[:, i, :], ACT.Square, accum_out=ms[:, i:i + 1]).then_inc(sq, 1)
                act.wait_ge(sq, i + 1)
            act.wait_ge(vch, 1)
            act.activation(rt[:], ms[:], ACT.Sqrt).then_inc(sd, 1)

        @block.vector
        def _(dve):
            link = linker(dve, vch)
            dve.wait_ge(sq, TT)
            link(dve.tensor_scalar(ms[:], ms[:], 1.0 / D, EPS, ALU.mult, ALU.add))
            dve.wait_ge(sd, 1)
            link(dve.reciprocal(rt[:], rt[:]))
            for i in range(TT):
                dve.tensor_scalar(xn[:, i, :], k.h[:, i, :], rt[:, i:i + 1], None, ALU.mult).then_inc(xnd, 1)
            for j in range(KD):
                dve.wait_ge(tr, j + 1)
                dve.tensor_scalar(hT[:, j, :], ps[j % 4][:], k.vec[:, wrow + j:wrow + j + 1], None, ALU.mult).then_inc(ev, 1)

        @block.tensor
        def _(pe):
            pe.wait_ge(xnd, TT)
            for j in range(KD):
                if j >= 4:
                    pe.wait_ge(ev, j - 3)
                for i in range(TT):
                    last = pe.transpose(ps[j % 4][:, i * P:(i + 1) * P], xn[:, i, j * P:(j + 1) * P], k.ident[:])
                last.then_inc(tr, 1)


def phase_project_2(nc, k, w, hT, b):
    L = w.first["in2"]
    jobs = []

    def feat(col, dst):
        n, c = L + col // 512, col % 512
        jobs.append((n, KD, lambda kk: w.tile(n)[:, kk, c:c + P], lambda kk: hT[:, kk, :], P, T, dst, None))

    def tok(col, dst):
        n, c = L + col // 512, col % 512
        for i in range(TT):
            jobs.append((n, KD, lambda kk, i=i: hT[:, kk, i * P:(i + 1) * P], lambda kk: w.tile(n)[:, kk, c:c + 256], P, 256, dst[:, i, :], None))

    for j in range(2):
        feat(j * P, b.qa[:, j, :])
    for j in range(2):
        feat(256 + j * P, b.ka[:, j, :])
    tok(512, b.va)
    for col, dst in ((768, b.qb), (1024, b.fb)):
        for j in range(2):
            feat(col + j * P, dst[:, j, :])
    tok(1280, b.ib)
    for col, dst in ((1536, b.gb), (1792, b.r), (2048, b.k), (2304, b.v)):
        for j in range(2):
            feat(col + j * P, dst[:, j, :])
    feat(2560, b.lo[:, 0, :])
    for col, dst in ((2688, b.xd), (2944, b.gd)):
        for j in range(2):
            feat(col + j * P, dst[:, j, :])
    with ExitStack() as st:
        project(nc, k, w, st, jobs, 8, None, (L + SLOTS, L + 9))


def phase_attention(nc, k, a, b, mixT):
    ps = k.ps
    ext_d = nc.dram_tensor("rel_ext", (4, 640), F32).ap()
    with ExitStack() as st:
        sem = lambda n: k.semaphore(n)
        sb = lambda n, s, d=F32: st.enter_context(nc.sbuf_tensor(n, s, d))
        ext = sb("rel_ext_sb", [4, 640])
        B = scratch(k, 4, 0, 4, T)
        R = scratch(k, 5, 0, 4, T)
        flip = scratch(k, 5, 2048, P)
        S = scratch(k, 4, 2048, 2, T)
        PT = scratch(k, 4, 3072, 2, T)
        mx, sm, rs = sb("a_max", [P, 16]), sb("a_sum", [P, 16]), sb("a_rs", [P, 16])
        ext_in, ext_ready, ext_out, b_in, b_ready = (sem(n) for n in ("ext_in", "ext_ready", "ext_out", "b_in", "b_ready"))
        flip_in, flipped, table = (sem(n) for n in ("flip_in", "flipped", "rel_table"))
        sc, biased, maxd, expd, normd, rsd, tr, ptd, pv, ev = (sem(n) for n in ("sc", "biased", "maxd", "expd", "normd", "rsd", "p_tr", "ptd", "pv", "a_ev"))
        block = st.enter_context(nc.Block())
        jobs = [(h, i) for h in range(4) for i in range(TT)]

        @block.sync
        def _(sp):
            sp.dma_start(ext[:, 255:639], a["attn_rel_bias_2"][0, :, 0:384]).then_inc(ext_in, 16)
            sp.dma_start(flip, a["const_flip"]).then_inc(flip_in, 16)
            sp.wait_ge(ext_ready, 1)
            sp.dma_start(ext_d, ext[:]).then_inc(ext_out, 16)
            sp.wait_ge(ext_out, 16)
            for h in range(4):
                src = bass.AP(tensor=ext_d.tensor, offset=h * 640, ap=[[1, P], [1, T]])
                sp.dma_start(R[:, h, :], src).then_inc(b_in, 16)

        @block.tensor
        def _(pe):
            def scores(j):
                h, i = jobs[j]
                r = slice(64 * (h % 2), 64 * (h % 2) + 64)
                if j >= 2:
                    pe.wait_ge(biased, j - 1)
                pe.matmul(ps[j % 2][:, 0:(i + 1) * P], b.qa[r, h // 2, i * P:(i + 1) * P], b.ka[r, h // 2, 0:(i + 1) * P], start=True, stop=True).then_inc(sc, 1)

            pe.wait_ge(flip_in, 16)
            pe.wait_ge(b_in, 64)
            for h in range(4):
                pe.matmul(ps[4 + h][:], flip, R[:, h, :], start=True, stop=True).then_inc(flipped, 1)
            scores(0)
            for j, (h, i) in enumerate(jobs):
                if j + 1 < len(jobs):
                    scores(j + 1)
                pe.wait_ge(normd, j + 1)
                if j >= 2:
                    pe.wait_ge(ptd, j - 1)
                for q in range(i + 1):
                    last = pe.transpose(ps[2 + j % 2][:, q * P:(q + 1) * P], S[:, j % 2, q * P:(q + 1) * P], k.ident[:])
                last.then_inc(tr, 1)
                pe.wait_ge(ptd, j + 1)
                r = slice(64 * (h % 2), 64 * (h % 2) + 64)
                for q in range(i + 1):
                    last = pe.matmul(ps[4 + h // 2][r, i * P:(i + 1) * P], b.va[:, q, h * 64:(h + 1) * 64], PT[:, j % 2, q * P:(q + 1) * P], start=q == 0, stop=q == i)
                last.then_inc(pv, 1)

        @block.vector
        def _(dve):
            dve.wait_ge(ext_in, 16)
            dve.tensor_copy(ext[:, 0:255], ext[:, 255:256].to_broadcast([4, 255])).then_inc(b_ready, 1)
            dve.wait_ge(b_ready, 1)
            dve.memset(ext[:, 639:640], 0.0).then_inc(ext_ready, 1)
            dve.wait_ge(table, 4)
            dve.memset(B[0:64, :, T - 64:T], -1e30).then_inc(b_ready, 1)
            dve.wait_ge(b_ready, 2)
            for j, (h, i) in enumerate(jobs):
                n = (i + 1) * P
                dve.wait_ge(sc, j + 1)
                if j >= 2:
                    dve.wait_ge(tr, j - 1)
                dve.scalar_tensor_tensor(out=S[:, j % 2, 0:n], in0=ps[j % 2][:, 0:n], scalar=64.0 ** -0.5, in1=B[:, h, T - n:T], op0=ALU.mult, op1=ALU.add).then_inc(biased, 1)
                dve.wait_ge(biased, j + 1)
                dve.tensor_reduce(mx[:, j:j + 1], S[:, j % 2, 0:n], AX_X, ALU.max, negate=True).then_inc(maxd, 1)
                dve.wait_ge(expd, j + 1)
                dve.reciprocal(rs[:, j:j + 1], sm[:, j:j + 1]).then_inc(rsd, 1)
                dve.wait_ge(rsd, j + 1)
                dve.tensor_scalar(S[:, j % 2, 0:n], S[:, j % 2, 0:n], rs[:, j:j + 1], None, ALU.mult).then_inc(normd, 1)

        @block.scalar
        def _(act):
            for h in range(4):
                act.wait_ge(flipped, h + 1)
                act.activation(B[:, h, :], ps[4 + h][:], ACT.Copy).then_inc(table, 1)
            for j, (h, i) in enumerate(jobs):
                n = (i + 1) * P
                act.wait_ge(maxd, j + 1)
                act.activation(S[:, j % 2, 0:n], S[:, j % 2, 0:n], ACT.Exp, bias=mx[:, j:j + 1], accum_out=sm[:, j:j + 1]).then_inc(expd, 1)
                act.wait_ge(tr, j + 1)
                if j >= 2:
                    act.wait_ge(pv, j - 1)
                act.activation(PT[:, j % 2, 0:n], ps[2 + j % 2][:, 0:n], ACT.Copy).then_inc(ptd, 1)
            act.wait_ge(pv, 16)
            for m in range(2):
                act.activation(mixT[:, m, :], ps[4 + m][:], ACT.Copy).then_inc(ev, 1)


def phase_lru(nc, k, a, b, mixT):
    ps = k.ps
    with ExitStack() as st:
        sem = lambda n: k.semaphore(n)
        sb = lambda n, s, d=F32: st.enter_context(nc.sbuf_tensor(n, s, d))
        wbd = sb("lru_w", [P, 2, 2, P])
        conv = scratch(k, 4, 0, 2, T)
        gr, gi = scratch(k, 4, 1024, 2, T), scratch(k, 4, 2048, 2, T)
        t1, t2, t3 = (scratch(k, 4, 3072 + 1024 * i, 2, T) for i in range(3))
        v2 = sb("lru_v", [P, 6, 2])
        wz, w_in, vch, ach, convd, mm, gates, lamr, tq, th, sqd, ge, ge1 = (sem(n) for n in (
            "lru_wz", "lru_w_in", "vch", "ach", "convd", "lru_mm", "gates", "lamr", "tq", "th", "sqd", "ge", "ge1"))
        ll = sem("l_e")
        block = st.enter_context(nc.Block())
        V = lambda name, j: k.vec[:, VEC[name] + j:VEC[name] + j + 1]
        V2 = lambda name: k.vec[:, VEC[name]:VEC[name] + 2]

        @block.gpsimd
        def _(pool):
            pool.memset(wbd[:], 0.0).then_inc(wz, 1)

        @block.sync
        def _(sp):
            sp.wait_ge(wz, 1)
            for g, src in enumerate((a["lru_wa_2"], a["lru_wx_2"])):
                for par in range(2):
                    r = slice(64 * par, 64 * par + 64)
                    sp.dma_start(wbd[r, g, :, 64 * par:64 * par + 64], src[0].rearrange("(m r) d e -> r d m e", r=2)[par]).then_inc(w_in, 16)

        @block.tensor
        def _(pe):
            pe.wait_ge(w_in, 64)
            pe.wait_ge(convd, 1)
            for g in range(2):
                for m in range(2):
                    last = pe.matmul(ps[2 * g + m][:], wbd[:, g, m, :], conv[:, m, :], start=True, stop=True)
                    last.then_inc(mm, 1)

        @block.scalar
        def _(act):
            act.activation(v2[:, 0, :], V2("lru_lambda_2"), ACT.Abs).then_inc(ll, 1)
            act.wait_ge(ll, 1)
            act.activation(v2[:, 1, :], v2[:, 0, :], ACT.Exp, scale=-1.0).then_inc(ll, 1)
            for g, (dst, bias) in enumerate(((gr, "lru_ba_2"), (gi, "lru_bx_2"))):
                for m in range(2):
                    act.wait_ge(mm, 2 * g + m + 1)
                    act.activation(dst[:, m, :], ps[2 * g + m][:], ACT.Sigmoid, bias=V(bias, m)).then_inc(gates, 1)
            act.wait_ge(tq, 2)
            act.activation(t1, gr, ACT.Tanh, scale=0.5).then_inc(th, 1)
            act.wait_ge(ge, 1)
            act.activation(t3, t3, ACT.Tanh, scale=0.7978845608028654).then_inc(ge1, 1)
            act.wait_ge(th, 1)
            act.activation(t2, t1, ACT.Sqrt).then_inc(sqd, 1)

        @block.vector
        def _(dve):
            link = linker(dve, vch)
            for m in range(2):
                x = b.xd[:, m, :]
                link(dve.tensor_scalar(conv[:, m, :], x, V("lru_conv_w_2", 6 + m), V("lru_conv_b_2", m), ALU.mult, ALU.add))
                for lag in (1, 2, 3):
                    link(dve.scalar_tensor_tensor(out=conv[:, m, lag:T], in0=x[:, 0:T - lag], scalar=V("lru_conv_w_2", 2 * (3 - lag) + m), in1=conv[:, m, lag:T], op0=ALU.mult, op1=ALU.add))
            dve.memset(v2[:, 5, :], 0.0).then_inc(convd, 1)
            dve.wait_ge(ll, 2)
            z, z2, acc = v2[:, 2, :], v2[:, 3, :], v2[:, 4, :]
            link(dve.tensor_scalar(z, v2[:, 1, :], 2.0, None, ALU.add))
            link(dve.reciprocal(z, z))
            link(dve.tensor_tensor(z, z, v2[:, 1, :], ALU.mult))
            link(dve.tensor_tensor(z2, z, z, ALU.mult))
            link(dve.tensor_scalar(acc, z2, 1.0 / 17, 1.0 / 15, ALU.mult, ALU.add))
            for n in (13, 11, 9, 7, 5, 3, 1):
                link(dve.tensor_tensor(acc, acc, z2, ALU.mult))
                link(dve.tensor_scalar(acc, acc, 1.0 / n, None, ALU.add))
            link(dve.tensor_tensor(acc, acc, z, ALU.mult))
            link(dve.tensor_scalar(z, V2("lru_lambda_2"), -1.0, 0.0, ALU.mult, ALU.max))
            link(dve.scalar_tensor_tensor(out=acc, in0=acc, scalar=2.0, in1=z, op0=ALU.mult, op1=ALU.add))
            link(dve.tensor_scalar(acc, acc, 8.0, None, ALU.mult))
            dve.wait_ge(gates, 4)
            for m in range(2):
                dve.tensor_scalar(gr[:, m, :], gr[:, m, :], v2[:, 4, m:m + 1], None, ALU.mult).then_inc(tq, 1)
            link(dve.tensor_tensor(gi, gi, conv, ALU.mult))
            link(dve.tensor_tensor(t3, b.gd[:], b.gd[:], ALU.mult))
            link(dve.tensor_scalar(t3, t3, 0.044715, 1.0, ALU.mult, ALU.add))
            dve.tensor_tensor(t3, t3, b.gd[:], ALU.mult).then_inc(ge, 1)
            dve.wait_ge(sqd, 1)
            link(dve.tensor_scalar(conv, t1, 1.0, None, ALU.add))
            link(dve.reciprocal(conv, conv))
            link(dve.tensor_scalar(t1, t1, -1.0, 1.0, ALU.mult, ALU.add))
            link(dve.tensor_tensor(t1, t1, conv, ALU.mult))
            link(dve.scalar_tensor_tensor(out=t2, in0=t2, scalar=2.0, in1=conv, op0=ALU.mult, op1=ALU.mult))
            link(dve.tensor_tensor(t2, t2, gi, ALU.mult))
            for m in range(2):
                last = dve.tensor_tensor_scan(gr[:, m, :], t1[:, m, :], t2[:, m, :], 0.0, ALU.mult, ALU.add)
                link(last)
            dve.wait_ge(ge1, 1)
            link(dve.scalar_tensor_tensor(out=t3, in0=t3, scalar=1.0, in1=b.gd[:], op0=ALU.add, op1=ALU.mult))
            link(dve.scalar_tensor_tensor(out=mixT[:, 6:8, :], in0=t3, scalar=0.5, in1=gr, op0=ALU.mult, op1=ALU.mult))


def phase_out_2(nc, k, a, w, mixT):
    ps = k.ps
    with ExitStack() as st:
        sem = lambda n: k.semaphore(n)
        mm = sem("o2_mm")
        post = post_norm(nc, k, st, "_mix", a["norm_mix_post_2"][0])
        block = st.enter_context(nc.Block())

        @block.tensor
        def _(pe):
            for half in range(2):
                n = w.first["out2"] + half
                w.wait(pe, n)
                for i in range(TT):
                    for kk in range(KD):
                        last = pe.matmul(ps[2 * i + half][:], mixT[:, kk, i * P:(i + 1) * P], w.tile(n)[:, kk, :], start=kk == 0, stop=kk == KD - 1)
                    last.then_inc(mm, 1)
                pe.wait_ge(mm, 4 * half + 4)
                pe.sem_inc(w.used, 1)

        block.scalar(lambda act: post.scalar(act, mm, lambda j: TT * (j % 2) + j // 2 + 1))
        block.vector(lambda dve: post.vector(dve))
        block.sync(lambda sp: post.sync(sp))


class post_norm:

    def __init__(self, nc, k, st, tag, wrow):
        sem = lambda n: k.semaphore(n + tag)
        sb = lambda n, s, d=F32: st.enter_context(nc.sbuf_tensor(n + tag, s, d))
        self.k, self.wrow = k, wrow
        self.w = sb("post_w", [P, D])
        self.junk = sb("post_junk", [P, 512])
        self.tmp = sb("post_tmp", [P, 2, 512])
        self.ms, self.rt = sb("post_ms", [P, 2 * TT]), sb("post_rt", [P, TT])
        self.w_in, self.sq, self.vch, self.sd, self.done = (sem(n) for n in ("post_w_in", "post_sq", "post_vch", "post_sd", "post_done"))

    def sync(self, sp):
        sp.dma_start(self.w[:], self.wrow.rearrange("(o d) -> o d", o=1).to_broadcast([P, D])).then_inc(self.w_in, 16)

    def scalar(self, act, ready, count):
        for j in range(2 * TT):
            act.wait_ge(ready, count(j))
            act.activation(self.junk[:], self.k.ps[j][:], ACT.Square, accum_out=self.ms[:, j:j + 1]).then_inc(self.sq, 1)
            act.wait_ge(self.sq, j + 1)
        act.wait_ge(self.vch, 2)
        act.activation(self.rt[:], self.rt[:], ACT.Sqrt).then_inc(self.sd, 1)

    def vector(self, dve):
        link = linker(dve, self.vch)
        dve.wait_ge(self.sq, 2 * TT)
        v = self.ms[:].rearrange("p (i s) -> p i s", s=2)
        link(dve.tensor_tensor(self.rt[:], v[:, :, 0], v[:, :, 1], ALU.add))
        link(dve.tensor_scalar(self.rt[:], self.rt[:], 1.0 / D, EPS, ALU.mult, ALU.add))
        dve.wait_ge(self.sd, 1)
        link(dve.reciprocal(self.rt[:], self.rt[:]))
        dve.wait_ge(self.w_in, 16)
        for j in range(2 * TT):
            i, cols = j // 2, slice((j % 2) * 512, (j % 2) * 512 + 512)
            link(dve.scalar_tensor_tensor(out=self.tmp[:, j % 2, :], in0=self.k.ps[j][:], scalar=self.rt[:, i:i + 1], in1=self.w[:, cols], op0=ALU.mult, op1=ALU.mult))
            dve.tensor_tensor(self.k.h[:, i, cols], self.k.h[:, i, cols], self.tmp[:, j % 2, :], ALU.add).then_inc(self.done, 1)
        dve.wait_ge(self.done, 2 * TT)


def phase_mlp_up(nc, k, a, w, hT, hid):
    ps = k.ps
    L = w.first["mlp1"]
    with ExitStack() as st:
        sem = lambda n: k.semaphore(n)
        tmp = st.enter_context(nc.sbuf_tensor("relu_tmp", [P, 2, 512], F32))
        mm, rl, sqd = sem("up_mm"), sem("relu"), sem("relu_sq")
        block = st.enter_context(nc.Block())

        @block.sync
        def _(sp):
            w.load(sp, L + SLOTS, L + 8 + SLOTS)

        @block.tensor
        def _(pe):
            for j in range(32):
                n = L + j // 4
                w.wait(pe, n)
                if j >= 8:
                    pe.wait_ge(rl, j - 7)
                for kk in range(KD):
                    last = pe.matmul(ps[j % 8][:], w.tile(n)[:, kk, (j % 4) * P:(j % 4 + 1) * P], hT[:, kk, :], start=kk == 0, stop=kk == KD - 1)
                last.then_inc(mm, 1)
                if j % 4 == 3:
                    pe.wait_ge(mm, j + 1)
                    pe.sem_inc(w.used, 1)

        @block.scalar
        def _(act):
            for j in range(32):
                act.wait_ge(mm, j + 1)
                if j >= 2:
                    act.wait_ge(sqd, j - 1)
                act.activation(tmp[:, j % 2, :], ps[j % 8][:], ACT.Relu).then_inc(rl, 1)

        @block.vector
        def _(dve):
            for j in range(32):
                dve.wait_ge(rl, j + 1)
                dve.tensor_tensor(hid[:, j, :], tmp[:, j % 2, :], tmp[:, j % 2, :], ALU.mult).then_inc(sqd, 1)


def phase_mlp_down(nc, k, a, w, hid, out):
    ps = k.ps
    L = w.first["mlp2"]
    with ExitStack() as st:
        sem = lambda n: k.semaphore(n)
        mm, out_done = sem("down_mm"), sem("out_done")
        post = post_norm(nc, k, st, "_mlp", a["norm_mlp_post_2"][0])
        block = st.enter_context(nc.Block())

        @block.tensor
        def _(pe):
            for g in range(8):
                w.wait(pe, L + g)
                for i in range(TT):
                    for half in range(2):
                        for q in range(4):
                            last = pe.matmul(ps[2 * i + half][:], hid[:, 4 * g + q, i * P:(i + 1) * P], w.tile(L + g)[:, q, half * 512:(half + 1) * 512],
                                             start=g == 0 and q == 0, stop=g == 7 and q == 3)
                        if g == 7:
                            last.then_inc(mm, 1)
                if g < 7:
                    last.then_inc(mm, 1)
                    pe.wait_ge(mm, g + 1)
                    pe.sem_inc(w.used, 1)

        @block.sync
        def _(sp):
            post.sync(sp)
            w.load(sp, L + SLOTS, L + 8)
            for i in range(TT):
                sp.wait_ge(post.done, 2 * i + 2)
                sp.dma_start(out[0, i * P:(i + 1) * P, :], k.h[:, i, :]).then_inc(out_done, 16)
            sp.wait_ge(out_done, 16 * TT)

        block.scalar(lambda act: post.scalar(act, mm, lambda j: 8 + j))
        block.vector(lambda dve: post.vector(dve))


def second_block(nc, k, a, w, out):
    with ExitStack() as s1:
        sb = lambda n, s, d=F32: s1.enter_context(nc.sbuf_tensor(n, s, d))
        b = Names()
        b.r, b.k, b.v, b.qb, b.fb, b.gb, b.xd, b.gd, b.qa, b.ka = (
            sb("b_" + name, [P, 2, T]) for name in ("r", "k", "v", "qb", "fb", "gb", "xd", "gd", "qa", "ka"))
        b.lo = sb("b_lo", [P, 1, T])
        b.va, b.ib = sb("b_va", [P, TT, 256]), sb("b_ib", [P, TT, 256])
        with ExitStack() as s2:
            hT = s2.enter_context(nc.sbuf_tensor("hT_2", [P, KD, T], F32))
            with ExitStack() as s3:
                phase_norm_turn(nc, k, "_mix", VEC["norm_mix_pre_2"], hT, None)
            phase_project_2(nc, k, w, hT, b)
        mixT = sb("mixT_2", [P, KD, T])
        phase_attention(nc, k, a, b, mixT)
        phase_lru(nc, k, a, b, mixT)
        phase_hgrn(nc, k, a, b, mixT)
        phase_rwkv(nc, k, a, b, mixT)
        phase_out_2(nc, k, a, w, mixT)
    with ExitStack() as s1:
        sb = lambda n, s, d=F32: s1.enter_context(nc.sbuf_tensor(n, s, d))
        hid = sb("hid", [P, 32, T])
        with ExitStack() as s2:
            hT = s2.enter_context(nc.sbuf_tensor("hT_3", [P, KD, T], F32))
            phase_norm_turn(nc, k, "_mlp", VEC["norm_mlp_pre_2"], hT, hid, lambda sp: w.load(sp, w.first["mlp1"], w.first["mlp1"] + SLOTS))
            phase_mlp_up(nc, k, a, w, hT, hid)
        phase_mlp_down(nc, k, a, w, hid, out)


def phase_hgrn(nc, k, a, b, mixT):
    ps = k.ps
    LEVELS = [32, 16, 8, 4, 2, 1, 0]
    qt = [scratch(k, 0, 2048 * i, 2, 2, T) for i in range(2)]
    kt = [scratch(k, 0, 4096 + 1024 * i, 2, T) for i in range(2)]
    E, C = scratch(k, 0, 6144, 2 * T), scratch(k, 0, 7168, 2 * T)
    A = scratch(k, 4, 0, TT, 4, P)
    qc = scratch(k, 4, 2048, 2, 2, T)
    kd = scratch(k, 4, 4096, 2, T)
    kdt = scratch(k, 4, 5120, TT, 256)
    lf = scratch(k, 4, 6144, 2 * T)
    S = scratch(k, 4, 7168, XCH, 2, 64)
    with ExitStack() as st:
        sem = lambda n: k.semaphore(n)
        sb = lambda n, s, d=F32: st.enter_context(nc.sbuf_tensor(n, s, d))
        masks = sb("hg_masks", [P, 7, P], I32)
        scanmask = sb("hg_scan", [P, T])
        decay = sb("hg_decay", [P, 2, XCH])
        ones64 = sb("hg_ones64", [P, P])
        flat = lambda t: t[:].rearrange("p m t -> p (m t)")
        c_in, vch, ach, pch, lfd, keyd, sgd, cd, d0, ed = (sem(n) for n in ("c_in", "vch", "ach", "pch", "lfd", "keyd", "sgd", "cum_d", "d_first", "e_d"))
        qd, kdn, mm, cp, e64, kdd, tr, trd, u, sd = (sem(n) for n in ("q_d", "k_d", "lev_mm", "lev_cp", "e64", "kd_d", "hg_tr", "hg_trd", "hg_u", "hg_s"))
        o, sq, mn, msum, root, gsig, qcd, zero, fin = (sem(n) for n in ("hg_o", "hg_sq", "hg_mean", "hg_msum", "hg_root", "hg_gsig", "hg_qc", "hg_zero", "hg_fin"))
        block = st.enter_context(nc.Block())

        @block.sync
        def _(sp):
            sp.dma_start(masks[:], a["const_level_masks"]).then_inc(c_in, 16)
            sp.dma_start(ones64[:], a["const_ones64"]).then_inc(c_in, 16)

        @block.scalar
        def _(act):
            link = linker(act, ach)
            link(act.activation(C, flat(b.fb), ACT.Abs))
            link(act.activation(C, C, ACT.Exp, scale=-1.0))
            act.activation(C, C, ACT.Ln, bias=1.0).then_inc(lfd, 1)
            act.wait_ge(keyd, 1)
            link(act.activation(b.fb[:], b.fb[:], ACT.Sigmoid, scale=-1.0))
            act.activation(kt[0], b.qb[:], ACT.Sigmoid).then_inc(sgd, 1)
            act.activation(kd, b.gb[:], ACT.Sigmoid).then_inc(gsig, 1)
            for j, s in enumerate(LEVELS[:-1]):
                act.wait_ge(d0, j + 1)
                v = E.rearrange("p (n a s) -> p n a s", a=2, s=s)
                cv = C.rearrange("p (n a s) -> p n a s", a=2, s=s)
                act.activation(v[:, :, 0, :], v[:, :, 0, :], ACT.Exp).then_inc(ed, 1)
                act.activation(v[:, :, 1, :], cv[:, :, 1, :], ACT.Exp).then_inc(ed, 1)
            act.wait_ge(d0, 7)
            act.activation(E, E, ACT.Exp).then_inc(e64, 1)
            act.activation(decay[:], C.rearrange("p (m n c) -> p m n c", m=2, c=CH)[:, :, :, CH - 1], ACT.Exp).then_inc(e64, 1)
            act.wait_ge(e64, 2)
            act.activation(C, C, ACT.Exp).then_inc(e64, 1)
            for i in range(TT):
                act.wait_ge(tr, i + 1)
                act.activation(kdt[:, i, :], ps[4 + i % 2][:, 0:256], ACT.Copy).then_inc(trd, 1)
            for m in range(2):
                act.wait_ge(o, m + 1)
                act.activation(kt[m][:, 0, :], ps[m][:], ACT.Square).then_inc(sq, 1)
            act.wait_ge(msum, 2)
            for m in range(2):
                act.activation(kt[m][:, 1, :], kt[m][:, 1, :], ACT.Sqrt).then_inc(root, 1)

        @block.gpsimd
        def _(pool):
            pool.memset(A, 0.0).then_inc(zero, 1)
            pool.memset(qc, 0.0).then_inc(zero, 1)
            pool.memset(qt[1], 0.0).then_inc(zero, 1)
            pool.wait_ge(sgd, 1)
            for j, s in enumerate(LEVELS):
                if j >= 2:
                    pool.wait_ge(mm, 4 * (j - 1))
                if j == 0:
                    pool.wait_ge(qd, 1)
                if s:
                    pool.wait_ge(ed, 2 * j + 2)
                    pool.tensor_tensor(kt[j % 2].rearrange("p m t -> p (m t)"), flat(b.fb), E, ALU.mult).then_inc(kdn, 1)
                else:
                    pool.tensor_copy(kt[j % 2], b.fb[:]).then_inc(kdn, 1)

        @block.vector
        def _(dve):
            link = linker(dve, vch)
            dve.memset(qt[0], 0.0).then_inc(zero, 1)
            dve.wait_ge(lfd, 1)
            dve.scalar_tensor_tensor(out=lf, in0=flat(b.fb), scalar=0.0, in1=C, op0=ALU.min, op1=ALU.subtract).then_inc(keyd, 1)
            dve.wait_ge(sgd, 1)
            dve.wait_ge(keyd, 1)
            dve.tensor_tensor(b.qb[:], b.qb[:], kt[0], ALU.mult).then_inc(qd, 1)
            dve.wait_ge(qd, 1)
            dve.wait_ge(zero, 4)
            dve.wait_ge(gsig, 1)
            link(dve.tensor_tensor(b.gb[:], b.gb[:], kd, ALU.mult))

            def cumulate(s):
                link(dve.memset(scanmask[:], 1.0))
                link(dve.memset(scanmask[:, ::s], 0.0))
                for m in range(2):
                    last = dve.tensor_tensor_scan(C[:, m * T:(m + 1) * T], scanmask[:], lf[:, m * T:(m + 1) * T], 0.0, ALU.mult, ALU.add)
                    link(last)

            def prepare(j):
                s = LEVELS[j]
                if s:
                    if j >= 1:
                        dve.wait_ge(kdn, j)
                    cumulate(s)
                    v = E.rearrange("p (n a s) -> p n a s", a=2, s=s)
                    cv = C.rearrange("p (n a s) -> p n a s", a=2, s=s)
                    dve.tensor_tensor(v[:, :, 0, :], cv[:, :, 0, s - 1:s].to_broadcast([P, T // s, s]), cv[:, :, 0, :], ALU.subtract).then_inc(d0, 1)
                    dve.wait_ge(ed, 2 * j + 2)
                if j >= 2:
                    dve.wait_ge(mm, 4 * (j - 1))
                for par in range(2):
                    r = slice(64 * par, 64 * par + 64)
                    if s:
                        dve.tensor_tensor(qt[j % 2][r, :, par, :], b.qb[r, :, :], E[r, :].rearrange("p (m t) -> p m t", m=2), ALU.mult).then_inc(qd, 1)
                    else:
                        dve.tensor_copy(qt[j % 2][r, :, par, :], b.qb[r, :, :]).then_inc(qd, 1)
                dve.wait_ge(qd, 1 + 2 * j + 2)

            dve.wait_ge(c_in, 32)
            prepare(0)
            for j in range(len(LEVELS)):
                if j + 1 < len(LEVELS):
                    prepare(j + 1)
                for i in range(TT):
                    dve.wait_ge(mm, 4 * j + i + 1)
                    if j >= 1:
                        dve.wait_ge(cp, 4 * (j - 1) + i + 1)
                    dve.copy_predicated(A[:, i, :, :], masks[:, j:j + 1, :].to_broadcast([P, 4, P]), ps[i][:].rearrange("p (h t) -> p h t", h=4)).then_inc(cp, 1)
            dve.wait_ge(kdn, 7)
            cumulate(CH)
            cv = C.rearrange("p (n c) -> p n c", c=CH)
            dve.tensor_tensor(E.rearrange("p (n c) -> p n c", c=CH), cv[:, :, CH - 1:CH].to_broadcast([P, 2 * XCH, CH]), cv, ALU.subtract).then_inc(d0, 1)
            dve.wait_ge(e64, 3)
            dve.tensor_tensor(kd, b.fb[:], E.rearrange("p (m t) -> p m t", m=2), ALU.mult).then_inc(kdd, 1)
            for par in range(2):
                r = slice(64 * par, 64 * par + 64)
                dve.tensor_tensor(qc[r, :, par, :], b.qb[r, :, :], C[r, :].rearrange("p (m t) -> p m t", m=2), ALU.mult).then_inc(qcd, 1)
            link(dve.memset(S[:, 0, :, :], 0.0))
            for n in range(XCH - 1):
                dve.wait_ge(u, n + 1)
                if n >= 1:
                    dve.wait_ge(sd, 2 * n)
                for m in range(2):
                    dve.scalar_tensor_tensor(out=S[:, n + 1, m, :], in0=S[:, n, m, :], scalar=decay[:, m, n:n + 1], in1=ps[6 + n % 2][:, m * 64:(m + 1) * 64], op0=ALU.mult, op1=ALU.add).then_inc(sd, 1)
            for m in range(2):
                dve.wait_ge(mn, m + 1)
                dve.tensor_scalar(kt[m][:, 1, :], ps[2 + m][:], EPS, None, ALU.add).then_inc(msum, 1)
            for m in range(2):
                dve.wait_ge(root, m + 1)
                link(dve.reciprocal(kt[m][:, 1, :], kt[m][:, 1, :]))
                c = VEC["hgrn_norm_2"] + m
                link(dve.scalar_tensor_tensor(out=kt[m][:, 1, :], in0=ps[m][:], scalar=k.vec[:, c:c + 1], in1=kt[m][:, 1, :], op0=ALU.mult, op1=ALU.mult))
                dve.tensor_tensor(mixT[:, 2 + m, :], kt[m][:, 1, :], b.gb[:, m, :], ALU.mult).then_inc(fin, 1)
            dve.wait_ge(fin, 2)

        @block.tensor
        def _(pe):
            for j in range(len(LEVELS)):
                pe.wait_ge(qd, 1 + 2 * j + 2)
                pe.wait_ge(kdn, j + 1)
                for i in range(TT):
                    if j >= 1:
                        pe.wait_ge(cp, 4 * (j - 1) + i + 1)
                    cols = slice(i * P, (i + 1) * P)
                    for h in range(4):
                        last = pe.matmul(ps[i][:, h * P:(h + 1) * P], kt[j % 2][:, h // 2, cols], qt[j % 2][:, h // 2, h % 2, cols], start=True, stop=True)
                    last.then_inc(mm, 1)
            pe.wait_ge(kdd, 1)
            for i in range(TT):
                if i >= 2:
                    pe.wait_ge(trd, i - 1)
                for m in range(2):
                    last = pe.transpose(ps[4 + i % 2][:, m * P:(m + 1) * P], kd[:, m, i * P:(i + 1) * P], k.ident[:])
                last.then_inc(tr, 1)
            pe.wait_ge(trd, TT)
            for n in range(XCH - 1):
                if n >= 2:
                    pe.wait_ge(sd, 2 * (n - 1))
                r = slice(64 * (n % 2), 64 * (n % 2) + 64)
                for h in range(4):
                    last = pe.matmul(ps[6 + n % 2][64 * (h % 2):64 * (h % 2) + 64, (h // 2) * 64:(h // 2) * 64 + 64],
                                     kdt[r, n // 2, h * 64:(h + 1) * 64], b.ib[r, n // 2, h * 64:(h + 1) * 64], start=True, stop=True)
                last.then_inc(u, 1)
            pe.wait_ge(cp, 28)
            pe.wait_ge(sd, 2 * (XCH - 1))
            pe.wait_ge(qcd, 2)
            for m in range(2):
                for h in (2 * m, 2 * m + 1):
                    rows = slice(64 * (h % 2), 64 * (h % 2) + 64)
                    for i in range(TT):
                        pe.matmul(ps[m][rows, i * P:(i + 1) * P], b.ib[:, i, h * 64:(h + 1) * 64], A[:, i, h, :], start=True, stop=False, skip_group_check=True)
                        for n in (2 * i, 2 * i + 1):
                            last = pe.matmul(ps[m][rows, n * CH:(n + 1) * CH], S[:, n, m, :], qc[:, m, h % 2, n * CH:(n + 1) * CH], start=False, stop=True, skip_group_check=True)
                last.then_inc(o, 1)
            for m in range(2):
                pe.wait_ge(sq, m + 1)
                pe.matmul(ps[2 + m][:], ones64[:], kt[m][:, 0, :], start=True, stop=True).then_inc(mn, 1)


def phase_rwkv(nc, k, a, b, mixT):
    x = Names()
    x.alp, x.rhp = scratch(k, 0, 0, 2, 2, T), scratch(k, 0, 2048, 2, 2, T)
    x.be, x.ka = scratch(k, 0, 4096, 2, T), scratch(k, 0, 5120, 2, T)
    x.LT = scratch(k, 0, 6144, TT, 4, P)
    x.T, x.TT, x.Z, x.Loff = (scratch(k, 4, 2048 * i, TT, 4, P) for i in range(4))
    x.al = scratch(k, 4, 4096, 2, T)
    tok = lambda t: t[:].rearrange("p m t -> p (m t)").rearrange("p (i c) -> p i c", i=TT)
    x.c = b.ka
    x.Bf, x.Kf = b.gd, b.ka
    x.vt, x.Bt, x.Kt = tok(b.fb), b.ib, b.va
    x.PQ = x.T
    x.Arb, x.Ark = scratch(k, 0, 0, TT, 4, P), x.LT
    x.MT = x.Loff.rearrange("p i h c -> p (i h c)").rearrange("p (n m c) -> p n m c", n=XCH, m=2)
    x.N = b.xd[:].rearrange("p m t -> p (m t)").rearrange("p (n m c) -> p n m c", n=XCH, m=2)
    x.S = b.qb[:].rearrange("p m t -> p (m t)").rearrange("p (n m c) -> p n m c", n=XCH, m=2)
    with ExitStack() as s1:
        sb = lambda n, s, d=F32: s1.enter_context(nc.sbuf_tensor(n, s, d))
        x.RHS = sb("rw_rhs", [P, TT, 4, P])
        x.ones64 = sb("rw_ones64", [P, P])
        x.Wc = sb("rw_wc", [P, 2, XCH])
        x.tri = sb("rw_tri", [P, 2, P], I32)
        rwkv_features(nc, k, a, b, x)
        rwkv_pairs(nc, k, a, b, x)
        rwkv_solve(nc, k, a, b, x)
        rwkv_states(nc, k, a, b, x)
        rwkv_outputs(nc, k, a, b, x, mixT)


def rwkv_features(nc, k, a, b, x):
    ps = k.ps
    e1, e2, e3, e4 = (scratch(k, 4, 1024 * i, 2, T) for i in range(4))
    with ExitStack() as st:
        sem = lambda n: k.semaphore(n)
        sb = lambda n, s, d=F32: st.enter_context(nc.sbuf_tensor(n, s, d))
        wl = sb("rw_lowrank", [P, 256])
        scanmask = sb("rw_scan", [P, T])
        w_in, vch, ach, xs, lod, mm, lwd, ad, gd, sq, nmm, nsd, bon, bmm, cc, ee = (sem(n) for n in (
            "rw_w_in", "vch", "ach", "xs", "lo_d", "rw_mm", "lw_d", "a_d", "g_d", "kk_sq", "kk_mm", "kk_sd", "bon", "bon_mm", "c_d", "e_d"))
        block = st.enter_context(nc.Block())
        V = lambda name, j=0: k.vec[:, VEC[name] + j:VEC[name] + j + 1]

        @block.sync
        def _(sp):
            sp.dma_start(wl[0:32, :], a["rwkv_w2_2"][0]).then_inc(w_in, 16)
            sp.dma_start(wl[32:64, :], a["rwkv_a2_2"][0]).then_inc(w_in, 16)
            sp.dma_start(wl[64:P, :], a["rwkv_g2_2"][0]).then_inc(w_in, 16)
            sp.dma_start(x.ones64[:], a["const_ones64"]).then_inc(w_in, 16)
            sp.dma_start(x.tri[:], a["const_tri"]).then_inc(w_in, 16)

        @block.tensor
        def _(pe):
            pe.wait_ge(w_in, 80)
            pe.wait_ge(lod, 2)
            for q, r in enumerate((slice(0, 32), slice(32, 64), slice(64, P))):
                for m in range(2):
                    pe.matmul(ps[2 * q + m][:], wl[r, m * P:(m + 1) * P], b.lo[r, 0, :], start=True, stop=True).then_inc(mm, 1)
            pe.wait_ge(sq, 1)
            for m in range(2):
                pe.matmul(ps[6 + m][:], x.ones64[:], b.qa[:, m, :], start=True, stop=True).then_inc(nmm, 1)
            pe.wait_ge(bon, 1)
            for m in range(2):
                pe.matmul(ps[m][:], x.ones64[:], b.gd[:, m, :], start=True, stop=True).then_inc(bmm, 1)

        @block.scalar
        def _(act):
            act.wait_ge(xs, 1)
            act.activation(b.lo[0:32, 0, :], b.lo[0:32, 0, :], ACT.Tanh).then_inc(lod, 1)
            act.activation(b.lo[64:P, 0, :], b.lo[64:P, 0, :], ACT.Sigmoid).then_inc(lod, 1)
            for m in range(2):
                act.wait_ge(mm, m + 1)
                act.activation(b.qb[:, m, :], ps[m][:], ACT.Sigmoid, bias=V("rwkv_w0_2", m)).then_inc(lwd, 1)
            for m in range(2):
                act.wait_ge(mm, m + 3)
                act.activation(b.fb[:, m, :], ps[2 + m][:], ACT.Sigmoid, bias=V("rwkv_a0_2", m)).then_inc(ad, 1)
            for m in range(2):
                act.wait_ge(mm, m + 5)
                act.activation(b.gb[:, m, :], ps[4 + m][:], ACT.Copy).then_inc(gd, 1)
            for m in range(2):
                act.wait_ge(nmm, m + 1)
                act.activation(b.gd[:, m, :], ps[6 + m][:], ACT.Sqrt, scale=float(RW_HD)).then_inc(nsd, 1)
            act.wait_ge(cc, 1)
            act.activation(e1, x.c[:], ACT.Exp).then_inc(ee, 1)
            act.activation(e3, x.c[:], ACT.Exp, scale=-1.0).then_inc(ee, 1)
            act.activation(x.Wc[:], x.c[:, :, CH - 1::CH], ACT.Exp).then_inc(ee, 1)
            act.wait_ge(cc, 2)
            act.activation(e2, e2, ACT.Exp).then_inc(ee, 1)
            act.wait_ge(cc, 3)
            act.activation(e4, e4, ACT.Exp).then_inc(ee, 1)

        @block.vector
        def _(dve):
            link = linker(dve, vch)
            for j, (t, n) in enumerate(((b.lo, 1), (b.r, 2), (b.k, 2), (b.v, 2))):
                mu = (6, 0, 2, 4)[j]
                d = b.qa
                link(dve.tensor_tensor(d[:, 0:n, 1:T], t[:, :, 0:T - 1], t[:, :, 1:T], ALU.subtract))
                link(dve.tensor_scalar(d[:, 0:n, 0:1], t[:, :, 0:1], -1.0, None, ALU.mult))
                for m in range(n):
                    last = dve.scalar_tensor_tensor(out=t[:, m, :], in0=d[:, m, :], scalar=V("rwkv_mu_2", mu + m), in1=t[:, m, :], op0=ALU.mult, op1=ALU.add)
                    if j == 0:
                        last.then_inc(xs, 1)
                        dve.wait_ge(xs, 1)
                    else:
                        link(last)
            for m in range(2):
                link(dve.tensor_scalar(b.xd[:, m, :], b.k[:, m, :], V("rwkv_k_k_2", m), None, ALU.mult))
            dve.tensor_tensor(b.qa[:], b.xd[:], b.xd[:], ALU.mult).then_inc(sq, 1)
            dve.wait_ge(lwd, 2)
            link(dve.tensor_scalar(b.qb[:], b.qb[:], -0.6065306597126334, None, ALU.mult))
            link(dve.memset(scanmask[:], 1.0))
            link(dve.memset(scanmask[:, ::CH], 0.0))
            for m in range(2):
                last = dve.tensor_tensor_scan(x.c[:, m, :], scanmask[:], b.qb[:, m, :], 0.0, ALU.mult, ALU.add)
                if m == 0:
                    link(last)
                else:
                    last.then_inc(cc, 1)
            dve.wait_ge(cc, 1)
            dve.tensor_tensor(e2, x.c[:], b.qb[:], ALU.subtract).then_inc(cc, 1)
            for m in range(2):
                cv = x.c[:, m, :].rearrange("p (n c) -> p n c", c=CH)
                last = dve.tensor_tensor(e4[:, m, :].rearrange("p (n c) -> p n c", c=CH), cv[:, :, CH - 1:CH].to_broadcast([P, XCH, CH]), cv, ALU.subtract)
                if m == 0:
                    link(last)
                else:
                    last.then_inc(cc, 1)
            dve.wait_ge(nsd, 2)
            link(dve.tensor_scalar(b.gd[:], b.gd[:], 1e-12, None, ALU.max))
            link(dve.reciprocal(b.gd[:], b.gd[:]))
            link(dve.tensor_tensor(b.xd[:], b.xd[:], b.gd[:], ALU.mult))
            dve.wait_ge(ad, 2)
            for m in range(2):
                link(dve.tensor_scalar(b.gd[:, m, :], b.fb[:, m, :], -1.0, V("rwkv_k_a_2", m), ALU.add, ALU.mult))
            link(dve.scalar_tensor_tensor(out=b.k[:], in0=b.gd[:], scalar=1.0, in1=b.k[:], op0=ALU.add, op1=ALU.mult))
            for m in range(2):
                last = dve.scalar_tensor_tensor(out=b.gd[:, m, :], in0=b.r[:, m, :], scalar=V("rwkv_r_k_2", m), in1=b.k[:, m, :], op0=ALU.mult, op1=ALU.mult)
                if m == 0:
                    link(last)
                else:
                    last.then_inc(bon, 1)
            link(dve.tensor_tensor(b.fb[:], b.fb[:], b.xd[:], ALU.mult))
            for m in range(2):
                dve.wait_ge(bmm, m + 1)
                link(dve.scalar_tensor_tensor(out=b.qa[:, m, :], in0=ps[m][:], scalar=float(RW_HD), in1=b.v[:, m, :], op0=ALU.mult, op1=ALU.mult))
            link(dve.memset(x.alp, 0.0))
            link(dve.memset(x.rhp, 0.0))
            dve.wait_ge(ee, 5)
            link(dve.scalar_tensor_tensor(out=x.al, in0=b.xd[:], scalar=-1.0, in1=e2, op0=ALU.mult, op1=ALU.mult))
            for par in range(2):
                r = slice(64 * par, 64 * par + 64)
                link(dve.tensor_copy(x.alp[r, :, par, :], x.al[r, :, :]))
                link(dve.tensor_tensor(x.rhp[r, :, par, :], b.r[r, :, :], e1[r, :, :], ALU.mult))
            link(dve.tensor_tensor(x.be, b.fb[:], e3, ALU.mult))
            link(dve.tensor_tensor(x.ka, b.k[:], e3, ALU.mult))
            link(dve.tensor_tensor(x.Bf[:], b.fb[:], e4, ALU.mult))
            link(dve.tensor_tensor(x.Kf[:], b.k[:], e4, ALU.mult))


def rwkv_pairs(nc, k, a, b, x):
    ps = k.ps
    Lak = x.Loff
    with ExitStack() as st:
        sem = lambda n: k.semaphore(n)
        tr, trd, lt, ltd, lak, lakd, rv, rvd, z = (sem(n) for n in ("p_tr", "p_trd", "p_lt", "p_ltd", "p_lak", "p_lakd", "p_rv", "p_rvd", "p_zero"))
        block = st.enter_context(nc.Block())

        @block.gpsimd
        def _(pool):
            pool.memset(x.LT, 0.0).then_inc(z, 1)
            pool.memset(Lak, 0.0).then_inc(z, 1)

        @block.tensor
        def _(pe):
            for i in range(TT):
                cols = slice(i * P, (i + 1) * P)
                if i >= 1:
                    pe.wait_ge(trd, 4 * i)
                for q, t in enumerate((x.al, x.Bf, x.Kf, b.v)):
                    for m in range(2):
                        last = pe.transpose(ps[q][:, m * P:(m + 1) * P], t[:, m, cols], k.ident[:])
                    last.then_inc(tr, 1)
                if i >= 1:
                    pe.wait_ge(ltd, i)
                    pe.wait_ge(lakd, i)
                for bank, lhs, s in ((4, x.be, lt), (5, x.ka, lak)):
                    for h in range(4):
                        last = pe.matmul(ps[bank][:, h * P:(h + 1) * P], lhs[:, h // 2, cols], x.alp[:, h // 2, h % 2, cols], start=True, stop=True)
                    last.then_inc(s, 1)
                pe.wait_ge(lakd, i + 1)
                pe.wait_ge(trd, 4 * i + 4)
                if i >= 1:
                    pe.wait_ge(rvd, i)
                for h in range(4):
                    last = pe.matmul(ps[6][:, h * 64:(h + 1) * 64], Lak[:, i, h, :], x.vt[:, i, h * 64:(h + 1) * 64], start=True, stop=True)
                last.then_inc(rv, 1)

        @block.scalar
        def _(act):
            for i in range(TT):
                for q, dst in enumerate((x.RHS[:, i, :, 0:64], x.Bt[:, i, :], x.Kt[:, i, :], x.vt[:, i, :])):
                    act.wait_ge(tr, 4 * i + q + 1)
                    src = ps[q][:, 0:256]
                    if q == 0:
                        src = src.rearrange("p (h c) -> p h c", h=4)
                    act.activation(dst, src, ACT.Copy).then_inc(trd, 1)
                act.wait_ge(rv, i + 1)
                act.activation(x.RHS[:, i, :, 64:P], ps[6][:, 0:256].rearrange("p (h c) -> p h c", h=4), ACT.Copy).then_inc(rvd, 1)

        @block.vector
        def _(dve):
            dve.wait_ge(z, 2)
            for i in range(TT):
                for bank, dst, s, d in ((4, x.LT, lt, ltd), (5, Lak, lak, lakd)):
                    dve.wait_ge(s, i + 1)
                    dve.copy_predicated(dst[:, i, :, :], x.tri[:, 0:1, :].to_broadcast([P, 4, P]), ps[bank][:].rearrange("p (h t) -> p h t", h=4)).then_inc(d, 1)


def rwkv_solve(nc, k, a, b, x):
    ps = k.ps
    with ExitStack() as st:
        sem = lambda n: k.semaphore(n)
        masks = st.enter_context(nc.sbuf_tensor("solve_masks", [P, 6, P], F32))
        c_in, init, off, z, zd, tz, tzd = (sem(n) for n in ("c_in", "init", "off", "z", "zd", "tz", "tzd"))
        block = st.enter_context(nc.Block())
        steps = [(l, i) for l in range(6) for i in range(TT)]

        @block.sync
        def _(sp):
            sp.dma_start(masks[:], a["const_level_masks_f"]).then_inc(c_in, 16)

        @block.gpsimd
        def _(pool):
            pool.wait_ge(c_in, 16)
            for n, (l, i) in enumerate(steps):
                if l >= 1:
                    pool.wait_ge(z, n - TT + 1)
                pool.tensor_tensor(x.Loff[:, i, :, :], x.LT[:, i, :, :], masks[:, 5 - l:6 - l, :].to_broadcast([P, 4, P]), ALU.mult).then_inc(off, 1)

        @block.tensor
        def _(pe):
            pe.wait_ge(init, 2)
            for n, (l, i) in enumerate(steps):
                def first(n):
                    l, i = steps[n]
                    pe.wait_ge(off, n + 1)
                    if l >= 1:
                        pe.wait_ge(tzd, 2 * (n - TT + 1))
                    if n >= 2:
                        pe.wait_ge(zd, n - 1)
                    for h in range(4):
                        last = pe.matmul(ps[n % 2][:, h * P:(h + 1) * P], x.Loff[:, i, h, :], x.T[:, i, h, :], start=True, stop=True)
                    last.then_inc(z, 1)
                if n == 0:
                    first(0)
                if n + 1 < len(steps):
                    first(n + 1)
                pe.wait_ge(zd, n + 1)
                if n >= 2:
                    pe.wait_ge(tzd, 2 * (n - 1))
                for h in range(4):
                    pe.matmul(ps[2 + n % 2][:, h * P:(h + 1) * P], x.TT[:, i, h, :], x.Z[:, i, h, :], start=True, stop=True)
                for h in range(4):
                    last = pe.matmul(ps[4 + n % 2][:, h * P:(h + 1) * P], x.Z[:, i, h, :], x.TT[:, i, h, :], start=True, stop=True)
                last.then_inc(tz, 1)

        @block.scalar
        def _(act):
            for n, (l, i) in enumerate(steps):
                act.wait_ge(z, n + 1)
                if l >= 1:
                    act.wait_ge(tz, n - TT + 1)
                act.activation(x.Z[:, i, :, :].rearrange("p h c -> p (h c)"), ps[n % 2][:], ACT.Copy).then_inc(zd, 1)

        @block.vector
        def _(dve):
            ident = k.ident[:, :].rearrange("p (o c) -> p o c", o=1).to_broadcast([P, 4 * TT, P])
            for t in (x.T, x.TT):
                dve.tensor_copy(t.rearrange("p i h c -> p (i h) c"), ident).then_inc(init, 1)
            dve.wait_ge(init, 2)
            for n, (l, i) in enumerate(steps):
                dve.wait_ge(tz, n + 1)
                if l >= 1:
                    dve.wait_ge(tzd, 2 * (n - TT + 1))
                for t, bank in ((x.T, 2), (x.TT, 4)):
                    v = t[:, i, :, :].rearrange("p h c -> p (h c)")
                    dve.tensor_tensor(v, v, ps[bank + n % 2][:], ALU.add).then_inc(tzd, 1)


def rwkv_states(nc, k, a, b, x):
    ps = k.ps
    with ExitStack() as st:
        sem = lambda n: k.semaphore(n)
        sb = lambda n, s, d=F32: st.enter_context(nc.sbuf_tensor(n, s, d))
        t1 = sb("rw_t1", [P, 2, 2, 64])
        zero, pq, pqd, ar, ard, mn, mnd, rr, rrd, sm, td, sd = (sem(n) for n in ("s_zero", "s_pq", "s_pqd", "s_ar", "s_ard", "s_mn", "s_mnd", "s_rr", "s_rrd", "s_mm", "s_td", "s_sd"))
        block = st.enter_context(nc.Block())

        @block.gpsimd
        def _(pool):
            pool.memset(x.Arb, 0.0).then_inc(zero, 1)
            pool.memset(x.Ark, 0.0).then_inc(zero, 1)
            pool.memset(x.MT, 0.0).then_inc(zero, 1)
            pool.memset(x.S[:, 0, :, :], 0.0).then_inc(zero, 1)

        @block.tensor
        def _(pe):
            for i in range(TT):
                if i >= 2:
                    pe.wait_ge(pqd, i - 1)
                for h in range(4):
                    last = pe.matmul(ps[i % 2][:, h * P:(h + 1) * P], x.TT[:, i, h, :], x.RHS[:, i, h, :], start=True, stop=True)
                last.then_inc(pq, 1)
            for i in range(TT):
                cols = slice(i * P, (i + 1) * P)
                if i >= 1:
                    pe.wait_ge(ard, 2 * i)
                for bank, lhs in ((2, x.be), (3, x.ka)):
                    for h in range(4):
                        last = pe.matmul(ps[bank][:, h * P:(h + 1) * P], lhs[:, h // 2, cols], x.rhp[:, h // 2, h % 2, cols], start=True, stop=True)
                    last.then_inc(ar, 1)
            pe.wait_ge(pqd, TT)
            for n in range(XCH - 1):
                if n >= 2:
                    pe.wait_ge(mnd, 3 * (n - 1))
                r, i = slice(64 * (n % 2), 64 * (n % 2) + 64), n // 2
                bank = ps[4 + n % 2]
                for h in range(4):
                    o, hc = slice(64 * (h % 2), 64 * (h % 2) + 64), slice(64 * h, 64 * h + 64)
                    c = (h // 2) * 64
                    pe.matmul(bank[o, c:c + 64], x.PQ[r, i, h, 0:64], x.Bt[r, i, hc], start=True, stop=True)
                    pe.matmul(bank[o, P + c:P + c + 64], x.Bt[r, i, hc], x.PQ[r, i, h, 64:P], start=True, stop=False)
                    last = pe.matmul(bank[o, P + c:P + c + 64], x.Kt[r, i, hc], x.vt[r, i, hc], start=False, stop=True)
                last.then_inc(mn, 1)
            pe.wait_ge(ard, 2 * TT)
            for h in range(4):
                o = slice(64 * (h % 2), 64 * (h % 2) + 64)
                for i in range(TT):
                    last = pe.matmul(ps[h // 2][o, i * P:(i + 1) * P], x.PQ[:, i, h, 0:64], x.Arb[:, i, h, :], start=True, stop=True)
                last.then_inc(rr, 1)
            pe.wait_ge(mnd, 3 * (XCH - 1))
            for n in range(XCH - 1):
                if n >= 1:
                    pe.wait_ge(sd, n)
                for m in range(2):
                    last = pe.matmul(ps[6 + n % 2][:, m * 64:(m + 1) * 64], x.MT[:, n, m, :], x.S[:, n, m, :], start=True, stop=True)
                last.then_inc(sm, 1)

        @block.scalar
        def _(act):
            for i in range(TT):
                act.wait_ge(pq, i + 1)
                act.activation(x.PQ[:, i, :, :].rearrange("p h c -> p (h c)"), ps[i % 2][:], ACT.Copy).then_inc(pqd, 1)
            act.wait_ge(zero, 4)
            for n in range(XCH - 1):
                act.wait_ge(mn, n + 1)
                bank = ps[4 + n % 2]
                for par in range(2):
                    o = slice(64 * par, 64 * par + 64)
                    act.activation(x.MT[o, n, :, o], bank[o, 0:P].rearrange("p (m c) -> p m c", m=2), ACT.Copy).then_inc(mnd, 1)
                act.activation(x.N[:, n, :, :], bank[:, P:2 * P].rearrange("p (m c) -> p m c", m=2), ACT.Copy).then_inc(mnd, 1)

        @block.vector
        def _(dve):
            dve.wait_ge(zero, 4)
            for i in range(TT):
                for q, (bank, dst) in enumerate(((2, x.Arb), (3, x.Ark))):
                    dve.wait_ge(ar, 2 * i + q + 1)
                    dve.copy_predicated(dst[:, i, :, :], x.tri[:, 1:2, :].to_broadcast([P, 4, P]), ps[bank][:].rearrange("p (h t) -> p h t", h=4)).then_inc(ard, 1)
            dve.wait_ge(rr, 4)
            dve.wait_ge(ar, 2 * TT)
            for h in range(4):
                o = slice(64 * (h % 2), 64 * (h % 2) + 64)
                v = x.rhp[o, h // 2, h % 2, :]
                dve.tensor_tensor(v, v, ps[h // 2][o, :], ALU.add).then_inc(rrd, 1)
            dve.wait_ge(mnd, 3 * (XCH - 1))
            for n in range(XCH - 1):
                if n >= 1:
                    dve.wait_ge(sd, n)
                for m in range(2):
                    dve.scalar_tensor_tensor(out=t1[:, n % 2, m, :], in0=x.S[:, n, m, :], scalar=x.Wc[:, m, n:n + 1], in1=x.N[:, n, m, :], op0=ALU.mult, op1=ALU.add).then_inc(td, 1)
                dve.wait_ge(td, 2 * n + 2)
                dve.wait_ge(sm, n + 1)
                dve.tensor_tensor(x.S[:, n + 1, :, :], t1[:, n % 2, :, :], ps[6 + n % 2][:, 0:P].rearrange("p (m c) -> p m c", m=2), ALU.add).then_inc(sd, 1)


def rwkv_outputs(nc, k, a, b, x, mixT):
    ps = k.ps
    y, sq = b.k, b.xd
    with ExitStack() as st:
        sem = lambda n: k.semaphore(n)
        o, yd, mean, cen, sqd, var, vard, root, vch = (sem(n) for n in ("y_mm", "y_d", "y_mean", "y_cen", "y_sq", "y_var", "y_vard", "y_root", "vch"))
        block = st.enter_context(nc.Block())
        V = lambda name, j=0: k.vec[:, VEC[name] + j:VEC[name] + j + 1]

        @block.tensor
        def _(pe):
            for h in range(4):
                r, m, bank = slice(64 * (h % 2), 64 * (h % 2) + 64), h // 2, ps[h // 2]
                for i in range(TT):
                    cols = slice(i * P, (i + 1) * P)
                    pe.matmul(bank[r, cols], x.PQ[:, i, h, 64:P], x.Arb[:, i, h, :], start=True, stop=False, skip_group_check=True)
                    pe.matmul(bank[r, cols], x.vt[:, i, h * 64:(h + 1) * 64], x.Ark[:, i, h, :], start=False, stop=False, skip_group_check=True)
                    for n in (2 * i, 2 * i + 1):
                        nc_ = slice(n * CH, (n + 1) * CH)
                        last = pe.matmul(bank[r, nc_], x.S[:, n, m, :], x.rhp[:, m, h % 2, nc_], start=False, stop=True, skip_group_check=True)
                last.then_inc(o, 1)
            for m in range(2):
                pe.wait_ge(yd, m + 1)
                pe.matmul(ps[2 + m][:], x.ones64[:], y[:, m, :], start=True, stop=True).then_inc(mean, 1)
            for m in range(2):
                pe.wait_ge(sqd, m + 1)
                pe.matmul(ps[4 + m][:], x.ones64[:], sq[:, m, :], start=True, stop=True).then_inc(var, 1)

        @block.scalar
        def _(act):
            for m in range(2):
                act.wait_ge(o, 2 * m + 2)
                act.activation(y[:, m, :], ps[m][:], ACT.Copy).then_inc(yd, 1)
            for m in range(2):
                act.wait_ge(cen, m + 1)
                act.activation(sq[:, m, :], y[:, m, :], ACT.Square).then_inc(sqd, 1)
            act.wait_ge(vard, 2)
            act.activation(sq[:], sq[:], ACT.Sqrt).then_inc(root, 1)

        @block.vector
        def _(dve):
            link = linker(dve, vch)
            for m in range(2):
                dve.wait_ge(mean, m + 1)
                dve.tensor_tensor(y[:, m, :], y[:, m, :], ps[2 + m][:], ALU.subtract).then_inc(cen, 1)
            for m in range(2):
                dve.wait_ge(var, m + 1)
                dve.tensor_scalar(sq[:, m, :], ps[4 + m][:], RW_HD * 1e-5, None, ALU.add).then_inc(vard, 1)
            dve.wait_ge(root, 1)
            link(dve.reciprocal(sq[:], sq[:]))
            link(dve.tensor_tensor(y[:], y[:], sq[:], ALU.mult))
            for m in range(2):
                link(dve.tensor_scalar(y[:, m, :], y[:, m, :], V("rwkv_ln_w_2", m), V("rwkv_ln_b_2", m), ALU.mult, ALU.add))
            link(dve.tensor_tensor(y[:], y[:], b.qa[:], ALU.add))
            link(dve.tensor_tensor(mixT[:, 4:6, :], y[:], b.gb[:], ALU.mult))


def build(nc, inputs):
    arrays, a = {}, {}
    for name, v in list(inputs.items()) + list(constants().items()):
        v = np.ascontiguousarray(v)
        arrays[f"in_{name}"] = v
        a[name] = nc.dram_tensor(f"in_{name}", v.shape, mybir.dt.from_np(v.dtype), kind="ExternalInput").ap()
    a["vec_views"] = {}
    for name, r in VEC_LIST:
        v = a[name]
        dims = " ".join("abcd"[:len(v.shape)])
        v = v.rearrange(f"{dims} -> ({dims})") if len(v.shape) > 1 else v
        a["vec_views"][name] = v.rearrange("(r p) -> r p", p=P)
    out = nc.dram_tensor("out_0", (1, T, D), F32, kind="ExternalOutput").ap()
    program(nc, a, out)
    return arrays


def kernel(**inputs):
    import concourse.bacc as bacc
    from concourse.bass_utils import run_bass_kernel_spmd
    nc = bacc.Bacc("TRN2", target_bir_lowering=False, num_devices=1)
    arrays = build(nc, inputs)
    return run_bass_kernel_spmd(nc, [arrays], core_ids=[0]).results[0]["out_0"]
```
